# Optimizing a Trainium2 kernel written in Bass

```python
import math
import jax, jax.numpy as jnp
from jax import lax
import numpy as np

D_MODEL = 2048
BATCH = 1
SEQ = 256
DEPTH = 2

N_A_LAYERS = DEPTH // 2
N_B_LAYERS = DEPTH - N_A_LAYERS
BLOCK_Q = 128
EPS = 1e-6

SB_HEADS = 16
SB_HEAD_DIM = D_MODEL // SB_HEADS

MLA_HEADS = 16
QK_NOPE = 128
QK_ROPE = 64
V_HEAD = 128
Q_LORA = 512
KV_LORA = 512
ROPE_BASE = 10000.0

PEER_HEADS = 8
N_KEYS = 128
N_EXPERTS = N_KEYS * N_KEYS
PEER_TOPK = 16
PEER_KEY_DIM = 256
PEER_HALF = PEER_KEY_DIM // 2
PEER_CHUNK = 128

kernel_name = 'hybrid_yoco_stickbreak_mla_peer'

def rmsnorm(x, g):
    xf = x.astype(jnp.float32)
    y = xf * lax.rsqrt(jnp.mean(xf * xf, axis=-1, keepdims=True) + EPS)
    return (y * g.astype(jnp.float32)).astype(x.dtype)

def rope(x, positions):
    r = x.shape[-1]
    inv_freq = ROPE_BASE ** (-jnp.arange(0, r, 2, dtype=jnp.float32) / r)
    ang = positions.astype(jnp.float32)[..., None] * inv_freq
    cos = jnp.cos(ang)[:, :, None, :]
    sin = jnp.sin(ang)[:, :, None, :]
    xf = x.astype(jnp.float32)
    x1, x2 = xf[..., : r // 2], xf[..., r // 2:]
    out = jnp.concatenate([x1 * cos - x2 * sin, x2 * cos + x1 * sin], axis=-1)
    return out.astype(x.dtype)

def stick_breaking_attention(h, w_qkv, w_o):
    b, s, _ = h.shape
    q, k, v = jnp.split(h @ w_qkv, 3, axis=-1)
    q = q.reshape(b, s, SB_HEADS, SB_HEAD_DIM)
    k = k.reshape(b, s, SB_HEADS, SB_HEAD_DIM)
    v = v.reshape(b, s, SB_HEADS, SB_HEAD_DIM)
    scale = SB_HEAD_DIM ** -0.5
    outs = []
    for i in range(s // BLOCK_Q):
        lo, hi = i * BLOCK_Q, (i + 1) * BLOCK_Q
        z = jnp.einsum('bqhd,bkhd->bhqk', q[:, lo:hi], k[:, :hi]).astype(jnp.float32) * scale
        causal = jnp.arange(hi)[None, :] < jnp.arange(lo, hi)[:, None]
        log_1m_beta = jnp.where(causal, jax.nn.log_sigmoid(-z), 0.0)
        tail = lax.cumsum(log_1m_beta, axis=3, reverse=True) - log_1m_beta
        a = jnp.where(causal, jnp.exp(jax.nn.log_sigmoid(z) + tail), 0.0)
        outs.append(jnp.einsum('bhqk,bkhd->bqhd', a.astype(v.dtype), v[:, :hi]))
    o = jnp.concatenate(outs, axis=1).reshape(b, s, SB_HEADS * SB_HEAD_DIM)
    return o @ w_o

def mla_shared_kv(x, positions, kv_norm_g, w_dkv, kv_latent_g, w_ukv):
    b, s, _ = x.shape
    h = rmsnorm(x, kv_norm_g)
    ckv = h @ w_dkv
    c = rmsnorm(ckv[..., :KV_LORA], kv_latent_g)
    k_rope = rope(ckv[..., None, KV_LORA:], positions)[:, :, 0, :]
    kv = (c @ w_ukv).reshape(b, s, MLA_HEADS, QK_NOPE + V_HEAD)
    return kv[..., :QK_NOPE], k_rope, kv[..., QK_NOPE:]

def mla_attention(h, positions, k_nope, k_rope, v, w_dq, q_latent_g, w_uq, w_o):
    b, s, _ = h.shape
    cq = rmsnorm(h @ w_dq, q_latent_g)
    q = (cq @ w_uq).reshape(b, s, MLA_HEADS, QK_NOPE + QK_ROPE)
    q_nope = q[..., :QK_NOPE]
    q_rope = rope(q[..., QK_NOPE:], positions)
    scale = (QK_NOPE + QK_ROPE) ** -0.5
    outs = []
    for i in range(s // BLOCK_Q):
        lo, hi = i * BLOCK_Q, (i + 1) * BLOCK_Q
        sc = (jnp.einsum('bqhd,bkhd->bhqk', q_nope[:, lo:hi], k_nope[:, :hi])
              + jnp.einsum('bqhr,bkr->bhqk', q_rope[:, lo:hi], k_rope[:, :hi])).astype(jnp.float32) * scale
        causal = jnp.arange(hi)[None, :] <= jnp.arange(lo, hi)[:, None]
        p = jax.nn.softmax(jnp.where(causal, sc, -jnp.inf), axis=-1)
        outs.append(jnp.einsum('bhqk,bkhd->bqhd', p.astype(v.dtype), v[:, :hi]))
    o = jnp.concatenate(outs, axis=1).reshape(b, s, MLA_HEADS * V_HEAD)
    return o @ w_o

def peer_ffn(h, w_q, keys_1, keys_2, expert_u, expert_v):
    b, s, d = h.shape
    q = (h @ w_q).reshape(b, s, PEER_HEADS, 2, PEER_HALF)
    s1 = jnp.einsum('bshd,hkd->bshk', q[..., 0, :], keys_1).astype(jnp.float32)
    s2 = jnp.einsum('bshd,hkd->bshk', q[..., 1, :], keys_2).astype(jnp.float32)
    v1, i1 = lax.top_k(s1, PEER_TOPK)
    v2, i2 = lax.top_k(s2, PEER_TOPK)
    cand_sc = (v1[..., :, None] + v2[..., None, :]).reshape(b, s, PEER_HEADS, PEER_TOPK * PEER_TOPK)
    cand_id = (i1[..., :, None] * N_KEYS + i2[..., None, :]).reshape(b, s, PEER_HEADS, PEER_TOPK * PEER_TOPK)
    top_sc, pos = lax.top_k(cand_sc, PEER_TOPK)
    ids = jnp.take_along_axis(cand_id, pos, axis=-1)
    g = jax.nn.softmax(top_sc, axis=-1).astype(h.dtype)
    n_sel = PEER_HEADS * PEER_TOPK
    n_chunks = (b * s) // PEER_CHUNK
    hc = h.reshape(n_chunks, PEER_CHUNK, d)
    idc = ids.reshape(n_chunks, PEER_CHUNK, n_sel)
    gc = g.reshape(n_chunks, PEER_CHUNK, n_sel)

    def chunk_fn(args):
        hx, idx, gx = args
        u = jnp.take(expert_u, idx, axis=0)
        act = jax.nn.gelu(jnp.einsum('ced,cd->ce', u, hx), approximate=False)
        vv = jnp.take(expert_v, idx, axis=0)
        return jnp.einsum('ce,ced->cd', gx * act, vv)

    out = lax.map(chunk_fn, (hc, idc, gc))
    return out.reshape(b, s, d)

def setup_inputs(seed: int = 0) -> dict:
    key = jax.random.key(seed)
    ks = jax.random.split(key, 24)

    def nrm(k, shape, scale):
        return jax.random.normal(k, shape, jnp.float32) * scale

    def gain(k, shape):
        return 1.0 + 0.01 * jax.random.normal(k, shape, jnp.float32)

    x = jax.random.normal(ks[0], (BATCH, SEQ, D_MODEL), jnp.float32)
    offsets = jax.random.randint(ks[1], (BATCH, 1), 0, 1024, dtype=jnp.int32)
    positions = (jnp.arange(SEQ, dtype=jnp.int32)[None, :] + offsets).astype(jnp.int32)
    return {
        'x': x,
        'positions': positions,
        'sb_norm_g': gain(ks[2], (N_A_LAYERS, D_MODEL)),
        'sb_w_qkv': nrm(ks[3], (N_A_LAYERS, D_MODEL, 3 * SB_HEADS * SB_HEAD_DIM), D_MODEL ** -0.5),
        'sb_w_o': nrm(ks[4], (N_A_LAYERS, SB_HEADS * SB_HEAD_DIM, D_MODEL), (SB_HEADS * SB_HEAD_DIM) ** -0.5),
        'kv_norm_g': gain(ks[5], (D_MODEL,)),
        'mla_w_dkv': nrm(ks[6], (D_MODEL, KV_LORA + QK_ROPE), D_MODEL ** -0.5),
        'mla_kv_latent_g': gain(ks[7], (KV_LORA,)),
        'mla_w_ukv': nrm(ks[8], (KV_LORA, MLA_HEADS * (QK_NOPE + V_HEAD)), KV_LORA ** -0.5),
        'mla_norm_g': gain(ks[9], (N_B_LAYERS, D_MODEL)),
        'mla_w_dq': nrm(ks[10], (N_B_LAYERS, D_MODEL, Q_LORA), D_MODEL ** -0.5),
        'mla_q_latent_g': gain(ks[11], (N_B_LAYERS, Q_LORA)),
        'mla_w_uq': nrm(ks[12], (N_B_LAYERS, Q_LORA, MLA_HEADS * (QK_NOPE + QK_ROPE)), Q_LORA ** -0.5),
        'mla_w_o': nrm(ks[13], (N_B_LAYERS, MLA_HEADS * V_HEAD, D_MODEL), (MLA_HEADS * V_HEAD) ** -0.5),
        'peer_norm_g': gain(ks[14], (DEPTH, D_MODEL)),
        'peer_w_q': nrm(ks[15], (DEPTH, D_MODEL, PEER_HEADS * PEER_KEY_DIM), D_MODEL ** -0.5),
        'peer_keys_1': nrm(ks[16], (DEPTH, PEER_HEADS, N_KEYS, PEER_HALF), PEER_HALF ** -0.5),
        'peer_keys_2': nrm(ks[17], (DEPTH, PEER_HEADS, N_KEYS, PEER_HALF), PEER_HALF ** -0.5),
        'peer_u': nrm(ks[18], (DEPTH, N_EXPERTS, D_MODEL), D_MODEL ** -0.5),
        'peer_v': nrm(ks[19], (DEPTH, N_EXPERTS, D_MODEL), PEER_HEADS ** -0.5),
        'final_norm_g': gain(ks[20], (D_MODEL,)),
    }

def reference(x, positions, sb_norm_g, sb_w_qkv, sb_w_o, kv_norm_g, mla_w_dkv, mla_kv_latent_g,
              mla_w_ukv, mla_norm_g, mla_w_dq, mla_q_latent_g, mla_w_uq, mla_w_o, peer_norm_g,
              peer_w_q, peer_keys_1, peer_keys_2, peer_u, peer_v, final_norm_g):
    k_nope = k_rope = v_shared = None
    for layer in range(DEPTH):
        if layer < N_A_LAYERS:
            x = x + stick_breaking_attention(rmsnorm(x, sb_norm_g[layer]), sb_w_qkv[layer], sb_w_o[layer])
        else:
            if layer == N_A_LAYERS:
                k_nope, k_rope, v_shared = mla_shared_kv(x, positions, kv_norm_g, mla_w_dkv,
                                                         mla_kv_latent_g, mla_w_ukv)
            j = layer - N_A_LAYERS
            x = x + mla_attention(rmsnorm(x, mla_norm_g[j]), positions, k_nope, k_rope, v_shared,
                                  mla_w_dq[j], mla_q_latent_g[j], mla_w_uq[j], mla_w_o[j])
        x = x + peer_ffn(rmsnorm(x, peer_norm_g[layer]), peer_w_q[layer], peer_keys_1[layer],
                         peer_keys_2[layer], peer_u[layer], peer_v[layer])
    return rmsnorm(x, final_norm_g)


_drawn_inputs = setup_inputs


def setup_inputs(seed=0):
    import zlib

    import numpy as np

    out = dict(_drawn_inputs(seed))
    spreads = {}
    factors = {'kv_norm_g': 7.324,
     'mla_kv_latent_g': 7.757,
     'mla_norm_g': 8.0,
     'mla_q_latent_g': 8.0,
     'final_norm_g': 5.738}
    for name, (base, spread) in spreads.items():
        noise = np.random.default_rng([zlib.crc32(name.encode()), seed]).standard_normal(out[name].shape)
        drawn = base * np.exp(spread * noise) if base else spread * noise
        out[name] = __import__('jax').numpy.asarray(drawn.astype(out[name].dtype))
    for name, factor in factors.items():
        out[name] = (out[name] * factor).astype(out[name].dtype)
    return out
```

```python
from contextlib import ExitStack

import numpy as np
import concourse.bass as bass
from concourse import mybir

F32 = mybir.dt.float32
F32R = mybir.dt.float32r
U32 = mybir.dt.uint32
I32 = mybir.dt.int32
F16 = mybir.dt.float16
ALU = mybir.AluOpType
ACT = mybir.ActivationFunctionType
AX = mybir.AxisListType

P = 128
D = 2048
S = 256
NC_TOK = S // P
KT = D // P
HEADS = 16
LORA = 512
LT = LORA // P
ROPE = 64
HALF_ROPE = ROPE // 2
PEER_HEADS = 8
TOPK = 16
NKEYS = 128
EPS = 1e-6
UNIT = 2048
HALF = UNIT // 2
RAW_SLOTS = 4
HALF_SLOTS = 4
LEAD = 2
TILES = NKEYS
GROUP = 4
GROUPS = TILES // GROUP
QUARTERS = D // 512
GROUP_UNITS = GROUP + QUARTERS
WQ_TILES = 32
BATCH = 8
BATCHES_PER_Q = S // BATCH
BATCHES = BATCHES_PER_Q * (TILES // WQ_TILES)
BODY_BATCHES = 4
PRE_BATCHES = BATCHES_PER_Q + BODY_BATCHES
BUILD_BODIES = (BATCHES - PRE_BATCHES) // BODY_BATCHES

SB_SCALE = 128 ** -0.5
MLA_SCALE = (128 + ROPE) ** -0.5
NEG = -1e30
WEIGHT_SCALE = 2.0 ** 15
N_CONSTS = 11
TWO_PI_PARTS = (6.28125, 0.0019350051879882812, 3.0199159795074593e-07)
PI_BELOW = 3.1415925
ROUND = 1.5 * 2.0 ** 23

PHASE_UNITS = [("qk", 32), ("v", 16), ("wo", 16), ("wq0", 16), ("peer0", 2 * TILES),
               ("c", 4), ("rope", 1), ("dq", 4), ("kn", 4), ("mv", 4), ("uqn", 4), ("uqr", 2),
               ("mwo", 16), ("wq1", 16), ("peer1", 2 * TILES)]
PHASE_A = [("norm_sb", 8), ("qk", 32), ("stick", 16), ("norm_p0", 8), ("wq0", 16), ("peer0", TILES),
           ("norm_kv", 8), ("norm_mla", 8), ("ct", 2), ("krt", 1), ("kn", 16), ("cqt", 2), ("uqn", 16),
           ("qrt", 4), ("mla", 16), ("norm_p1", 8), ("wq1", 16), ("peer1", TILES)]
PHASE_B = [("v", 4), ("stick", 16), ("wo", 4), ("peer0", GROUPS * QUARTERS), ("c", 1), ("rope", 1),
           ("dq", 1), ("mv", 4), ("uqr", 2), ("mla", 16), ("mwo", 4), ("peer1", GROUPS * QUARTERS)]
PHASE_C = [("stick", 16), ("wq0", 16), ("sel0", 2), ("peer0", BATCHES), ("mla", 16), ("wq1", 16),
           ("sel1", 2), ("peer1", BATCHES)]


def starts(table):
    out, n = {}, 0
    for name, count in table:
        out[name] = n
        n += count
    return out, n


U0, N_UNITS = starts(PHASE_UNITS)
A0, _ = starts(PHASE_A)
B0, _ = starts(PHASE_B)
C0, _ = starts(PHASE_C)
AF0, _ = starts([("norm_sb", 8), ("stick", 16), ("norm_p0", 8), ("norm_kv", 8), ("norm_mla", 8), ("ct", 2),
                 ("krt", 1), ("kn", 8), ("cqt", 2), ("uqn", 8), ("qrt", 4), ("mla", 16), ("norm_p1", 8)])
BF0, _ = starts([("stick", 16), ("mla", 16)])

G_SB, G_P0, G_KV, G_MLA, G_P1 = (KT * i for i in range(5))
G_LKV = 5 * KT
G_LQ = G_LKV + LT
N_GAINS = G_LQ + LT


def plus(base, it, step):
    return base if it is None else it * step + base


class Steps:

    def __init__(self, engine, semaphore):
        self.engine, self.semaphore, self.count = engine, semaphore, 0

    def do(self, instruction):
        instruction.then_inc(self.semaphore, 1)
        self.count += 1

    def sync(self):
        self.engine.wait_ge(self.semaphore, self.count)


def build_program(nc, x, positions, stream, keys, gains, final_g, inv_freq, out):
    with ExitStack() as ctx:
        def sem(name):
            return ctx.enter_context(nc.semaphore(name))

        def sb(name, shape, dt=F32):
            return ctx.enter_context(nc.sbuf_tensor(name, shape, dt))

        x_res = sb("x_res", [P, NC_TOK, D])
        act_t = sb("act_t", [P, KT, 2, S], F32R)
        raw = sb("raw", [P, RAW_SLOTS, UNIT])
        hi = sb("hi", [P, HALF_SLOTS, HALF], F32R)
        lo = sb("lo", [P, HALF_SLOTS, HALF], F32R)
        ident = sb("ident", [P, P])
        iota = sb("iota", [P, P])
        neg_upper = sb("neg_upper", [P, P])
        gain_t = sb("gain_t", [P, N_GAINS])
        eps_t = sb("eps_t", [P, 1])
        stat = sb("stat", [P, 16])
        cos_t = sb("cos_t", [P, NC_TOK, HALF_ROPE])
        sin_t = sb("sin_t", [P, NC_TOK, HALF_ROPE])

        KB = 1024
        arena_kb = 93
        arena_at = (nc.sbuf_base + 31) // 32 * 32
        sb("arena", [P, arena_kb * KB // 4])

        def place(name, kb, shape, dt=F32):
            size = 4 * int(np.prod(shape[1:]))
            assert kb * KB + size <= arena_kb * KB, name
            return nc.alloc_sbuf_tensor_at(name, shape, dt, offset=arena_at + int(kb * KB))

        xn = place("xn", 72, [P, NC_TOK, D])
        qk_t = place("qk_t", 0, [P, 2 * HEADS, S])
        v_tok = place("v_tok", 32, [P, NC_TOK, D])
        tri = place("tri", 48, [P, P])
        ones = place("ones", 48.5, [P, P])
        below = place("below", 49, [P, 3, P])
        LIVE = 3 * P
        st_l = place("st_l", 51, [P, 2, LIVE])
        st_sp = place("st_sp", 54, [P, 2, LIVE])
        st_spm = place("st_spm", 57, [P, 2, LIVE])
        st_arg = place("st_arg", 60, [P, 2, LIVE])
        st_e = place("st_e", 63, [P, 2, LIVE])
        st_a = place("st_a", 66, [P, 2, LIVE])
        qn_t = place("qn_t", 0, [P, HEADS, S])
        kn_t = place("kn_t", 16, [P, HEADS, S])
        mv_tok = place("mv_tok", 32, [P, NC_TOK, D])
        qr_t = place("qr_t", 48, [P, HEADS // 2, S])
        c_t = place("c_t", 56, [P, LT, 2, S], F32R)
        cq_t = place("cq_t", 64, [P, LT, 2, S], F32R)
        qr_tok = place("qr_tok", 72, [P, NC_TOK, HEADS * ROPE])
        rope_u = place("rope_u", 80, [P, 8 * HALF_ROPE])
        rope_v = place("rope_v", 81, [P, 8 * HALF_ROPE])
        c_tok = place("c_tok", 88, [P, NC_TOK, LORA])
        kr_tok = place("kr_tok", 92, [P, NC_TOK, 2 * ROPE])
        kr_t = place("kr_t", 92, [P, S])
        ml_s = place("ml_s", 72, [P, 2, LIVE])
        ml_p = place("ml_p", 75, [P, 2, LIVE])
        ml_pt = place("ml_pt", 78, [P, 2, LIVE])
        ml_stat = place("ml_stat", 81, [P, 2, 8])
        keys_sb = place("keys_sb", 0, [P, 2 * PEER_HEADS, NKEYS])
        pq_t = place("pq_t", 8, [P, 2, S])
        top_v = place("top_v", 10, [P, NC_TOK, PEER_HEADS, 2, TOPK])
        top_i = place("top_i", 12, [P, NC_TOK, PEER_HEADS, 2, TOPK], U32)
        top_f = place("top_f", 14, [P, NC_TOK, PEER_HEADS, 2, TOPK])
        cut = place("cut", 16, [P, NC_TOK, NKEYS])
        cand = place("cand", 17, [P, NC_TOK, TOPK * TOPK])
        cand_cut = place("cand_cut", 19, [P, NC_TOK, TOPK * TOPK])
        sel_v = place("sel_v", 21, [P, NC_TOK, PEER_HEADS, TOPK])
        sel_p = place("sel_p", 22, [P, NC_TOK, PEER_HEADS, TOPK], U32)
        pos_u = place("pos_u", 23, [P, 2, NC_TOK * P], U32)
        pos_f = place("pos_f", 25, [P, 2, NC_TOK * P])
        sel_f = place("sel_f", 27, [P, 3, NC_TOK, P])
        soft = place("soft", 30, [P, 4, NC_TOK * PEER_HEADS])
        match = place("match", 32, [P, P, TOPK])
        w_route = place("w_route", 0, [P, 2 * WQ_TILES, S])
        wa = place("wa", 64, [P, GROUP, 2, S], F32R)
        stage = place("stage", 72, [P, GROUP, S])
        iota_rep = place("iota_rep", 76, [P, P, BATCH], F16)
        hot2 = place("hot2", 78, [P, 2, P, BATCH], F16)
        hot1 = place("hot1", 82, [P, WQ_TILES, BATCH], F16)
        hot1g = place("hot1g", 83, [P, 2, 2, WQ_TILES, BATCH], F16)
        i1_t = place("i1_t", 85, [P, S], F16)
        i2_t = place("i2_t", 85.5, [P, S], F16)
        g_parts = place("g_parts", 86, [P, 2, S], F16)
        g_full = place("g_full", 87, [P, S])
        gain_row = place("gain_row", 0, [P, D])
        pos_i = place("pos_i", 0, [P, NC_TOK], I32)
        ang = place("ang", 1, [P, 6, NC_TOK * HALF_ROPE])
        invf = place("invf", 4, [P, HALF_ROPE])

        bank = [ctx.enter_context(nc.psum_tensor(f"bank{i}", [P, 512], F32)) for i in range(8)]
        ps_a = bank[0:2]
        ps_b = [bank[2:4], bank[4:6]]
        ps_c = bank[6:8]

        boot = sem("boot")
        x_in = sem("x_in")
        consts = sem("consts")
        raw_in = [sem(f"raw_in{i}") for i in range(RAW_SLOTS)]
        hi_ready = [sem(f"hi_ready{i}") for i in range(HALF_SLOTS)]
        lo_ready = [sem(f"lo_ready{i}") for i in range(HALF_SLOTS)]
        used = [sem(f"used{i}") for i in range(HALF_SLOTS)]
        a_full, a_free = sem("a_full"), sem("a_free")
        b_full, b_free = sem("b_full"), sem("b_free")
        c_full, c_free = sem("c_full"), sem("c_free")
        dve_step = sem("dve_step")
        act_step = sem("act_step")
        stds = sem("stds")
        xn_ready = sem("xn_ready")
        gain_hi = sem("gain_hi")
        angles = sem("angles")
        trig = sem("trig")
        st_log = sem("st_log")
        st_soft = sem("st_soft")
        st_masked = sem("st_masked")
        st_args = sem("st_args")
        st_exp = sem("st_exp")
        st_weights = sem("st_weights")
        ot_hi = sem("ot_hi")
        kr_ready = sem("kr_ready")
        qr_ready = sem("qr_ready")
        ml_masked = sem("ml_masked")
        ml_exp = sem("ml_exp")
        ml_norm = sem("ml_norm")
        keys_in = sem("keys_in")
        soft_in = sem("soft_in")
        soft_out = sem("soft_out")
        sel_ready = sem("sel_ready")
        sel_t_ready = sem("sel_t_ready")
        hot2_ready = sem("hot2_ready")
        hot1_ready = sem("hot1_ready")
        hot1g_ready = sem("hot1g_ready")
        gelu_done = sem("gelu_done")
        weighted = sem("weighted")
        wa_hi = sem("wa_hi")
        wa_lo = sem("wa_lo")
        final_ready = sem("final_ready")
        gain_row_in = sem("gain_row_in")
        stored = sem("stored")

        dve_consts = sem("dve_consts")
        GRANTED = 2

        def halves(n0, it, per):
            for j in range(2):
                h = 2 * n0 + j
                yield j, h % HALF_SLOTS, plus(h // HALF_SLOTS, it, 2 * per // HALF_SLOTS)

        def unit_done(engine, n0, it=None, per=0):
            *_, (_, s, k) = halves(n0, it, per)
            engine.wait_ge(used[s], k + 1)

        block = ctx.enter_context(nc.Block())

        @block.sync
        def _(sp):
            sp.dma_start(gain_t[:], gains).then_inc(boot, 16)
            for c in range(NC_TOK):
                sp.dma_start(x_res[:, c, :], x[c * P:(c + 1) * P, :]).then_inc(x_in, 16)
            sp.dma_start(pos_i[:], positions).then_inc(boot, 16)
            sp.dma_start(invf[:], inv_freq.to_broadcast([P, HALF_ROPE])).then_inc(boot, 16)

            def load(n0, it=None, first=False):
                if not first:
                    for j, s, k in halves(n0 - RAW_SLOTS, it, RAW_SLOTS):
                        sp.wait_ge(lo_ready[s], k + 1)
                slot = n0 % RAW_SLOTS
                sp.dma_start(raw[:, slot, :], stream[plus(n0, it, RAW_SLOTS)]).then_inc(raw_in[slot], 16)

            for n in range(RAW_SLOTS):
                load(n, first=True)
            rounds = N_UNITS // RAW_SLOTS
            with nc.sync.Fori(0, rounds - 1) as i:
                for n in range(RAW_SLOTS):
                    load(RAW_SLOTS + n, i)
            for n in range(rounds * RAW_SLOTS, N_UNITS):
                load(n)
            for c in range(NC_TOK):
                sp.wait_ge(final_ready, c + 1)
                sp.dma_start(out[c * P:(c + 1) * P, :], xn[:, c, :]).then_inc(stored, 16)
            sp.wait_ge(stored, 16 * NC_TOK)

        @block.gpsimd
        def _(pool):
            pool.memset(ident[:], 0.0).then_inc(consts, 1)
            pool.memset(neg_upper[:], 0.0).then_inc(consts, 1)
            pool.memset(tri[:], 1.0).then_inc(consts, 1)
            pool.memset(ones[:], 1.0).then_inc(consts, 1)
            pool.memset(below[:], 1.0).then_inc(consts, 1)
            pool.wait_ge(consts, 5)
            pool.affine_select(out=ident[:], in_=ident[:], compare_op=ALU.not_equal, fill=1.0, base=0,
                               pattern=[[-1, P]], channel_multiplier=1).then_inc(consts, 1)
            pool.affine_select(out=neg_upper[:], in_=neg_upper[:], compare_op=ALU.is_ge, fill=NEG, base=0,
                               pattern=[[-1, P]], channel_multiplier=1).then_inc(consts, 1)
            pool.affine_select(out=tri[:], in_=tri[:], compare_op=ALU.is_gt, fill=0.0, base=0,
                               pattern=[[-1, P]], channel_multiplier=1).then_inc(consts, 1)
            for b in (0, 2):
                pool.affine_select(out=below[:, b, :], in_=below[:, b, :], compare_op=ALU.is_gt, fill=0.0,
                                   base=0, pattern=[[1, P]], channel_multiplier=-1).then_inc(consts, 1)
            pool.iota(iota[:], pattern=[[1, P]], base=0, channel_multiplier=0,
                      allow_small_or_imprecise_dtypes=True).then_inc(consts, 1)

            def split_lo(n0, it=None, per=0):
                for j, s, k in halves(n0, it, per):
                    if s == HALF_SLOTS - 1 and n0 < N_UNITS:
                        pool.wait_ge(hi_ready[s], k + 1)
                        pool.tensor_tensor(lo[:, s, :], raw[:, n0 % RAW_SLOTS, j * HALF:(j + 1) * HALF],
                                           hi[:, s, :].bitcast(F32), ALU.subtract).then_inc(lo_ready[s], 1)

            def split_range(first, last):
                n = first
                rounds = (last - first) // RAW_SLOTS
                if rounds > 1:
                    with nc.gpsimd.Fori(0, rounds) as i:
                        for j in range(RAW_SLOTS):
                            split_lo(n + j, i, RAW_SLOTS)
                    n += rounds * RAW_SLOTS
                for m in range(n, last):
                    split_lo(m)

            def mask_head(h, src, dst, ready, freed, done):
                pool.wait_ge(ready, h + 1)
                if freed is not None and h >= 2:
                    pool.wait_ge(freed[0], freed[1] + h - 1)
                pool.tensor_tensor(dst[:, h % 2, :], src[:, h % 2, :],
                                   below[:].rearrange("p b q -> p (b q)"), ALU.mult).then_inc(done, 1)

            def weigh_hot1(layer, b, it=None):
                count = plus(layer * BATCHES + b, it, BODY_BATCHES)
                pool.wait_ge(hot1_ready, count + 1)
                pool.wait_ge(c_full, plus(C0[f"peer{layer}"] + b - 1, it, BODY_BATCHES))
                tok = (plus(b, it, BODY_BATCHES) % BATCHES_PER_Q) * BATCH
                for part in range(2):
                    g = g_parts[:, part, bass.ds(tok, BATCH)].unsqueeze(1)
                    pool.tensor_tensor(hot1g[:, b % 2, part, :, :], hot1[:],
                                       g.to_broadcast([P, WQ_TILES, BATCH]), ALU.mult).then_inc(hot1g_ready, 1)

            def peer(layer):
                base = U0[f"peer{layer}"]
                for j in range(GROUP):
                    split_lo(base + j + LEAD)
                pool.wait_ge(sel_t_ready, layer + 1)
                with nc.gpsimd.Fori(0, PRE_BATCHES // BODY_BATCHES) as i:
                    for b in range(BODY_BATCHES):
                        weigh_hot1(layer, b, i)
                for first, last, build in ((0, BUILD_BODIES, True), (BUILD_BODIES, GROUPS - 1, False)):
                    with nc.gpsimd.Fori(first, last) as i:
                        for j in range(GROUP_UNITS):
                            split_lo(base + GROUP + j + LEAD, i, GROUP_UNITS)
                            if build and j % 2 == 0:
                                weigh_hot1(layer, PRE_BATCHES + j // 2, i)
                for j in range(QUARTERS):
                    split_lo(base + 2 * TILES - QUARTERS + j + LEAD)

            split_range(0, U0["wo"] + LEAD)
            for h in range(HEADS + 1):
                if h < HEADS:
                    mask_head(h, st_sp, st_spm, st_soft, (c_full, C0["stick"]), st_masked)
                if h >= 1:
                    mask_head(h - 1, st_e, st_a, st_exp, (b_full, BF0["stick"]), st_weights)
            split_range(U0["wo"] + LEAD, U0["peer0"] + LEAD)
            peer(0)
            split_range(U0["c"] + LEAD, U0["peer1"] + LEAD)
            peer(1)

        @block.scalar
        def _(act):
            steps = Steps(act, act_step)

            def split_hi(n0, it=None, per=0):
                if n0 >= N_UNITS:
                    return
                slot = n0 % RAW_SLOTS
                act.wait_ge(raw_in[slot], plus(16 * (n0 // RAW_SLOTS + 1), it, 16 * per // RAW_SLOTS))
                for j, s, k in halves(n0, it, per):
                    if it is not None or k > 0:
                        act.wait_ge(used[s], k)
                    act.activation(hi[:, s, :], raw[:, slot, j * HALF:(j + 1) * HALF],
                                   ACT.Copy).then_inc(hi_ready[s], 1)

            def split_range(first, last):
                n = first
                rounds = (last - first) // RAW_SLOTS
                if rounds > 1:
                    with nc.scalar.Fori(0, rounds) as i:
                        for j in range(RAW_SLOTS):
                            split_hi(n + j, i, RAW_SLOTS)
                    n += rounds * RAW_SLOTS
                for m in range(n, last):
                    split_hi(m)

            def root_mean_square(k, rows, junk, width, col):
                for c in range(NC_TOK):
                    steps.do(act.activation(junk(c), rows(c), ACT.Square, accum_out=stat[:, col + c:col + c + 1]))
                steps.sync()
                act.activation(stat[:, col:col + NC_TOK], stat[:, col:col + NC_TOK], ACT.Sqrt,
                               bias=eps_t[:, 0:1], scale=1.0 / width).then_inc(stds, 1)

            def gains_hi(phase, k_tiles, col, dst):
                a0 = A0[phase]
                for f in range(k_tiles // 2):
                    act.wait_ge(a_full, AF0[phase] + f + 1)
                    for k in range(2):
                        kt = 2 * f + k
                        ins = act.activation(dst[:, kt, 0, :], ps_a[(a0 + f) % 2][:, k * S:(k + 1) * S], ACT.Copy,
                                             scale=gain_t[:, col + kt:col + kt + 1])
                    ins.then_inc(gain_hi, 1)

            def x_norm(k, b_end, phase, col):
                if b_end:
                    act.wait_ge(b_free, GRANTED + b_end)
                else:
                    act.wait_ge(x_in, 16 * NC_TOK)
                root_mean_square(k, lambda c: x_res[:, c, :], lambda c: xn[:, c, :], D, 0)
                gains_hi(phase, KT, col, act_t)

            def output_hi(h, phase):
                b0 = B0[phase]
                act.wait_ge(b_full, BF0[phase] + h + 1)
                act.activation(act_t[:, h, 0, :], ps_b[(b0 + h) % 2][0][:, 0:S], ACT.Copy).then_inc(ot_hi, 1)

            def peer(layer):
                base = U0[f"peer{layer}"]
                a0 = A0[f"peer{layer}"]

                def gelu(t, it=None):
                    act.wait_ge(a_free, plus(GRANTED + a0 + t + 1, it, GROUP))
                    act.activation(stage[:, t % GROUP, :], stage[:, t % GROUP, :], ACT.Gelu).then_inc(gelu_done, 1)

                def coefficients_hi(g, it=None):
                    act.wait_ge(weighted, plus(layer * TILES + GROUP * (g + 1), it, GROUP))
                    unit_done(act, base + GROUP - 1 + GROUP_UNITS * g, it, GROUP_UNITS)
                    act.activation(wa[:, :, 0, :], stage[:], ACT.Copy).then_inc(wa_hi, 1)

                act.preload_act_table_set("gelu_and_others")
                for j in range(GROUP):
                    split_hi(base + j + LEAD)
                    gelu(j)
                act.wait_ge(soft_in, layer + 1)
                act.activation(sel_f[:, 2, :, :], sel_f[:, 2, :, :], ACT.Exp).then_inc(soft_out, 1)
                act.preload_act_table_set("gelu_and_others")
                with nc.scalar.Fori(0, GROUPS - 1) as i:
                    coefficients_hi(0, i)
                    for j in range(GROUP_UNITS):
                        split_hi(base + GROUP + j + LEAD, i, GROUP_UNITS)
                        if j < GROUP:
                            gelu(GROUP + j, i)
                coefficients_hi(GROUPS - 1)
                for j in range(QUARTERS):
                    split_hi(base + 2 * TILES - QUARTERS + j + LEAD)

            def routing(layer):
                act.dma_start(keys_sb[:], keys[layer]).then_inc(keys_in, 16)
                split_range(U0[f"wq{layer}"] + LEAD, U0[f"peer{layer}"] + LEAD)

            act.wait_ge(boot, 48)
            act.wait_ge(dve_consts, 1)
            for m in range(LEAD):
                split_hi(m)
            x_norm(0, 0, "norm_sb", G_SB)
            act.wait_ge(angles, 1)
            act.activation(sin_t[:].rearrange("p c f -> p (c f)"), ang[:, 4, :], ACT.Sin).then_inc(trig, 1)
            act.activation(cos_t[:].rearrange("p c f -> p (c f)"), ang[:, 5, :], ACT.Sin).then_inc(trig, 1)
            split_range(LEAD, U0["wo"] + LEAD)

            act.preload_act_table_set("natural_log_exp_and_others")
            for h in range(HEADS + 2):
                if h < HEADS:
                    tmp = st_l[:, h % 2, :]
                    act.wait_ge(a_free, GRANTED + A0["stick"] + h + 1)
                    if h >= 2:
                        act.wait_ge(st_soft, h - 1)
                    steps.do(act.activation(tmp, st_arg[:, h % 2, :], ACT.Abs))
                    steps.sync()
                    steps.do(act.activation(tmp, tmp, ACT.Exp, scale=-1.0))
                    steps.sync()
                    act.activation(tmp, tmp, ACT.Ln, bias=1.0).then_inc(st_log, 1)
                if 1 <= h <= HEADS:
                    g = h - 1
                    act.wait_ge(st_args, g + 1)
                    if g >= 2:
                        act.wait_ge(st_weights, g - 1)
                    act.activation(st_e[:, g % 2, :], st_arg[:, g % 2, :], ACT.Exp).then_inc(st_exp, 1)
                if h >= 2:
                    output_hi(h - 2, "stick")
            split_range(U0["wo"] + LEAD, U0["wq0"] + LEAD)

            x_norm(1, B0["wo"] + 4, "norm_p0", G_P0)
            routing(0)
            peer(0)

            x_norm(2, B0["peer0"] + GROUPS * QUARTERS, "norm_kv", G_KV)
            split_range(U0["c"] + LEAD, U0["rope"] + 1 + LEAD)
            unit_done(act, U0["rope"])
            gains_hi("norm_mla", KT, G_MLA, act_t)
            unit_done(act, U0["c"] + 3)
            root_mean_square(3, lambda c: ps_b[B0["c"] % 2][c][:], lambda c: c_tok[:, c, :], LORA, 4)
            gains_hi("ct", LT, G_LKV, c_t)
            split_range(U0["dq"] + LEAD, U0["kn"] + LEAD)
            unit_done(act, U0["dq"] + 3)
            act.wait_ge(a_full, AF0["ct"] + 2)
            root_mean_square(4, lambda c: ps_b[B0["dq"] % 2][c][:], lambda c: c_tok[:, c, :], LORA, 8)
            split_range(U0["kn"] + LEAD, U0["uqn"] + LEAD)
            gains_hi("cqt", LT, G_LQ, cq_t)
            split_range(U0["uqn"] + LEAD, U0["mwo"] + LEAD)
            act.preload_act_table_set("exp_and_others")
            for h in range(HEADS + 2):
                if h < HEADS:
                    act.wait_ge(ml_masked, h + 1)
                    if h >= 2:
                        act.wait_ge(c_full, C0["mla"] + h - 1)
                    for c, (lo_col, hi_col) in enumerate(((0, P), (P, LIVE))):
                        ins = act.activation(ml_p[:, h % 2, lo_col:hi_col], ml_s[:, h % 2, lo_col:hi_col], ACT.Exp,
                                             bias=ml_stat[:, h % 2, 2 + c:3 + c], scale=MLA_SCALE,
                                             accum_out=ml_stat[:, h % 2, 4 + c:5 + c])
                    ins.then_inc(ml_exp, 1)
                if 1 <= h <= HEADS:
                    g = h - 1
                    act.wait_ge(c_full, C0["mla"] + g + 1)
                    if g >= 2:
                        act.wait_ge(b_full, BF0["mla"] + g - 1)
                    act.activation(ml_pt[:, g % 2, :], ps_c[(C0["mla"] + g) % 2][:, 0:LIVE],
                                   ACT.Copy).then_inc(c_free, 1)
                if h >= 2:
                    output_hi(h - 2, "mla")
            split_range(U0["mwo"] + LEAD, U0["wq1"] + LEAD)

            x_norm(5, B0["mwo"] + 4, "norm_p1", G_P1)
            routing(1)
            peer(1)

            act.wait_ge(b_free, GRANTED + B0["peer1"] + GROUPS * QUARTERS)
            act.dma_start(gain_row[:], final_g.to_broadcast([P, D])).then_inc(gain_row_in, 16)
            root_mean_square(6, lambda c: x_res[:, c, :], lambda c: xn[:, c, :], D, 0)

        @block.vector
        def _(dve):
            steps = Steps(dve, dve_step)

            def split_lo(n0, it=None, per=0):
                for j, s, k in halves(n0, it, per):
                    if s != HALF_SLOTS - 1 and n0 < N_UNITS:
                        dve.wait_ge(hi_ready[s], k + 1)
                        dve.tensor_tensor(lo[:, s, :], raw[:, n0 % RAW_SLOTS, j * HALF:(j + 1) * HALF],
                                          hi[:, s, :].bitcast(F32), ALU.subtract).then_inc(lo_ready[s], 1)

            def sum_halves(dst, idx):
                dve.tensor_reduce(dst, ps_a[idx % 2][:].rearrange("p (w t) -> p t w", w=2), AX.X,
                                  ALU.add).then_inc(a_free, 1)

            def scale_rows(k, rows, dst, col, done):
                dve.wait_ge(stds, k + 1)
                inv = stat[:, col + 2:col + 2 + NC_TOK]
                steps.do(dve.reciprocal(inv, stat[:, col:col + NC_TOK]))
                steps.sync()
                for c in range(NC_TOK):
                    ins = dve.tensor_scalar(dst(c), rows(c), stat[:, col + 2 + c:col + 3 + c], None, ALU.mult)
                    if c == NC_TOK - 1 and done is not None:
                        ins.then_inc(done, 1)

            gain_count = [0]

            def gains_lo(a0, k_tiles, col, dst):
                for f in range(k_tiles // 2):
                    gain_count[0] += 1
                    dve.wait_ge(gain_hi, gain_count[0])
                    for k in range(2):
                        kt = 2 * f + k
                        ins = dve.scalar_tensor_tensor(
                            out=dst[:, kt, 1, :], in0=ps_a[(a0 + f) % 2][:, k * S:(k + 1) * S],
                            scalar=gain_t[:, col + kt:col + kt + 1], in1=dst[:, kt, 0, :].bitcast(F32),
                            op0=ALU.mult, op1=ALU.subtract)
                    ins.then_inc(a_free, 1)

            def copy_block(idx, dst, col, last):
                unit_done(dve, last)
                for c in range(NC_TOK):
                    ins = dve.tensor_copy(dst[:, c, col:col + 512], ps_b[idx % 2][c][:])
                ins.then_inc(b_free, 1)

            def add_block(idx, col, last, it=None, per=0):
                unit_done(dve, last, it, per)
                for c in range(NC_TOK):
                    r = x_res[:, c, col:col + 512]
                    ins = dve.tensor_tensor(r, r, ps_b[idx % 2][c][:], ALU.add)
                ins.then_inc(b_free, 1)

            def output_lo(h, b0, count):
                dve.wait_ge(ot_hi, count + h + 1)
                dve.tensor_tensor(act_t[:, h, 1, :], ps_b[(b0 + h) % 2][0][:, 0:S],
                                  act_t[:, h, 0, :].bitcast(F32), ALU.subtract).then_inc(b_free, 1)

            def blocks(first, b0, n_blocks, store):
                for nb in range(n_blocks):
                    for j in range(4):
                        split_lo(first + 4 * nb + j + LEAD)
                    store(b0 + nb, 512 * nb, first + 4 * nb + 3)

            def rotate(src, dst, c, heads):
                def table(t):
                    return t[:, c, :].unsqueeze(1).to_broadcast([P, heads, HALF_ROPE])
                u = rope_u[:, 0:heads * HALF_ROPE].rearrange("p (h f) -> p h f", h=heads)
                v = rope_v[:, 0:heads * HALF_ROPE].rearrange("p (h f) -> p h f", h=heads)
                one, two = src[:, :, 0:HALF_ROPE], src[:, :, HALF_ROPE:ROPE]
                for x_, y_, where, op in ((one, two, 0, ALU.subtract), (two, one, HALF_ROPE, ALU.add)):
                    steps.do(dve.tensor_tensor(u, x_, table(cos_t), ALU.mult))
                    steps.do(dve.tensor_tensor(v, y_, table(sin_t), ALU.mult))
                    steps.sync()
                    steps.do(dve.tensor_tensor(dst[:, :, where:where + HALF_ROPE], u, v, op))
                    steps.sync()

            def top16(src, values, indices, cut_at, released=None):
                for c in range(NC_TOK):
                    steps.do(dve.max(values(c)[:, 0:8], src(c)))
                steps.sync()
                for c in range(NC_TOK):
                    steps.do(dve.match_replace(cut_at(c), values(c)[:, 0:8], src(c), -3e38))
                for c in range(NC_TOK):
                    ins = dve.max_index(indices(c)[:, 0:8], values(c)[:, 0:8], src(c))
                    if c == NC_TOK - 1 and released is not None:
                        ins.then_inc(released, 1)
                    else:
                        steps.do(ins)
                steps.sync()
                for c in range(NC_TOK):
                    steps.do(dve.max(values(c)[:, 8:16], cut_at(c)))
                steps.sync()
                for c in range(NC_TOK):
                    steps.do(dve.max_index(indices(c)[:, 8:16], values(c)[:, 8:16], cut_at(c)))

            def route_unit(layer, u):
                h, half = u // 2, u % 2
                idx = C0[f"wq{layer}"] + u
                dve.wait_ge(c_full, idx + 1)
                top16(lambda c: ps_c[idx % 2][:, c * P:(c + 1) * P], lambda c: top_v[:, c, h, half, :],
                      lambda c: top_i[:, c, h, half, :], lambda c: cut[:, c, :], c_free)
                if half == 0:
                    return
                steps.sync()
                for c in range(NC_TOK):
                    steps.do(dve.tensor_tensor(
                        cand[:, c, :].rearrange("p (a b) -> p a b", a=TOPK),
                        top_v[:, c, h, 0, :].unsqueeze(2).to_broadcast([P, TOPK, TOPK]),
                        top_v[:, c, h, 1, :].unsqueeze(1).to_broadcast([P, TOPK, TOPK]), ALU.add))
                steps.sync()
                top16(lambda c: cand[:, c, :], lambda c: sel_v[:, c, h, :], lambda c: sel_p[:, c, h, :],
                      lambda c: cand_cut[:, c, :])

            def finish_routing(layer):
                steps.sync()
                dve.wait_ge(c_free, GRANTED + C0[f"wq{layer}"] + 2 * PEER_HEADS)
                rows = sel_v[:].rearrange("p c h k -> p (c h) k")
                e = sel_f[:, 2, :, :].rearrange("p c (h k) -> p (c h) k", k=TOPK)
                n = NC_TOK * PEER_HEADS
                dve.tensor_tensor(e, rows, rows[:, :, 0:1].to_broadcast([P, n, TOPK]),
                                  ALU.subtract).then_inc(soft_in, 1)
                flat = sel_p[:].rearrange("p c h k -> p (c h k)")
                steps.do(dve.tensor_scalar(pos_u[:, 0, :], flat, 4, None, ALU.logical_shift_right))
                steps.do(dve.tensor_scalar(pos_u[:, 1, :], flat, TOPK - 1, None, ALU.bitwise_and))
                steps.do(dve.tensor_copy(top_f[:].rearrange("p c h w k -> p (c h w k)"),
                                         top_i[:].rearrange("p c h w k -> p (c h w k)")))
                steps.sync()
                steps.do(dve.tensor_copy(pos_f[:].rearrange("p w s -> p (w s)"),
                                         pos_u[:].rearrange("p w s -> p (w s)")))
                for w in range(2):
                    for c in range(NC_TOK):
                        steps.sync()
                        m4 = match[:].rearrange("p (h s) k -> p h s k", h=PEER_HEADS)
                        steps.do(dve.tensor_tensor(
                            match[:], pos_f[:, w, c * P:(c + 1) * P].unsqueeze(2).to_broadcast([P, P, TOPK]),
                            iota[:, 0:TOPK].unsqueeze(1).to_broadcast([P, P, TOPK]), ALU.is_equal))
                        steps.sync()
                        for h in range(PEER_HEADS):
                            steps.do(dve.tensor_tensor(
                                m4[:, h], m4[:, h], top_f[:, c, h, w, :].unsqueeze(1).to_broadcast([P, TOPK, TOPK]),
                                ALU.mult))
                        steps.sync()
                        steps.do(dve.tensor_reduce(sel_f[:, w, c, :], match[:], AX.X, ALU.add))
                dve.wait_ge(soft_out, layer + 1)
                steps.do(dve.tensor_reduce(soft[:, 0, 0:n], e, AX.X, ALU.add))
                steps.sync()
                steps.do(dve.reciprocal(soft[:, 1, 0:n], soft[:, 0, 0:n]))
                steps.sync()
                dve.tensor_tensor(e, e, soft[:, 1, 0:n].unsqueeze(2).to_broadcast([P, n, TOPK]),
                                  ALU.mult).then_inc(sel_ready, 1)
                c0 = C0[f"sel{layer}"]
                dve.wait_ge(c_full, c0 + 1)
                dve.tensor_copy(i1_t[:], ps_c[c0 % 2][:, 0:S])
                dve.tensor_copy(i2_t[:], ps_c[c0 % 2][:, S:2 * S]).then_inc(c_free, 1)
                dve.wait_ge(c_full, c0 + 2)
                dve.tensor_scalar(g_full[:], ps_c[(c0 + 1) % 2][:, 0:S], WEIGHT_SCALE, None,
                                  ALU.mult).then_inc(c_free, 1)
                dve.wait_ge(c_free, GRANTED + c0 + 2)
                steps.do(dve.tensor_copy(g_parts[:, 0, :], g_full[:]))
                steps.sync()
                dve.tensor_tensor(g_parts[:, 1, :], g_full[:], g_parts[:, 0, :], ALU.subtract).then_inc(sel_t_ready, 1)

            def peer(layer):
                base = U0[f"peer{layer}"]
                a0, b0, c0 = A0[f"peer{layer}"], B0[f"peer{layer}"], C0[f"peer{layer}"]
                done = layer * BATCHES

                def one_hots(b, it=None):
                    n = plus(b, it, BODY_BATCHES)
                    tok = (n % BATCHES_PER_Q) * BATCH
                    first = (n // BATCHES_PER_Q) * WQ_TILES
                    dve.wait_ge(c_full, plus(c0 + b - 1, it, BODY_BATCHES))
                    dve.tensor_tensor(hot2[:, b % 2, :, :], iota_rep[:],
                                      i2_t[:, bass.ds(tok, BATCH)].unsqueeze(1).to_broadcast([P, P, BATCH]),
                                      ALU.is_equal).then_inc(hot2_ready, 1)
                    if it is not None or done + b > 0:
                        dve.wait_ge(hot1g_ready, plus(2 * (done + b), it, 2 * BODY_BATCHES))
                    dve.tensor_tensor(hot1[:], iota_rep[:, bass.ds(first, WQ_TILES), :],
                                      i1_t[:, bass.ds(tok, BATCH)].unsqueeze(1).to_broadcast([P, WQ_TILES, BATCH]),
                                      ALU.is_equal).then_inc(hot1_ready, 1)

                def store_w(b, it=None):
                    n = plus(b, it, BODY_BATCHES)
                    tok = (n % BATCHES_PER_Q) * BATCH
                    slot = ((n // BATCHES_PER_Q) % 2) * WQ_TILES
                    dve.wait_ge(c_full, plus(c0 + b + 1, it, BODY_BATCHES))
                    dve.tensor_reduce(
                        w_route[:, bass.ds(slot, WQ_TILES), bass.ds(tok, BATCH)].rearrange("p i t -> p t i"),
                        ps_c[(c0 + b) % 2][:].rearrange("p (t w i) -> p t i w", w=2, i=WQ_TILES), AX.X,
                        ALU.add).then_inc(c_free, 1)

                def weigh(t, it=None, batches=None):
                    dve.wait_ge(gelu_done, plus(layer * TILES + t + 1, it, GROUP))
                    if batches is not None:
                        dve.wait_ge(c_free, batches)
                    tile = plus(t, it, GROUP) % (2 * WQ_TILES)
                    st = stage[:, t % GROUP, :].unsqueeze(1)
                    dve.scalar_tensor_tensor(out=st, in0=w_route[:, bass.ds(tile, 1), :], scalar=1 / WEIGHT_SCALE,
                                             in1=st, op0=ALU.mult, op1=ALU.mult).then_inc(weighted, 1)

                def coefficients_lo(g, it=None):
                    dve.wait_ge(wa_hi, plus(layer * GROUPS + g + 1, it, 1))
                    dve.tensor_tensor(wa[:, :, 1, :], stage[:], wa[:, :, 0, :].bitcast(F32),
                                      ALU.subtract).then_inc(wa_lo, 1)

                for j in range(GROUP):
                    split_lo(base + j + LEAD)
                    unit_done(dve, base + j)
                    sum_halves(stage[:, j, :], a0 + j)
                    if j == 0:
                        route_unit(layer, 2 * PEER_HEADS - 1)
                finish_routing(layer)
                steps.do(dve.tensor_copy(iota_rep[:], iota[:].unsqueeze(2).to_broadcast([P, P, BATCH])))
                steps.sync()
                one_hots(0)
                with nc.vector.Fori(0, BATCHES_PER_Q // BODY_BATCHES) as i:
                    for b in range(BODY_BATCHES):
                        one_hots(b + 1, i)
                        store_w(b, i)
                for j in range(GROUP):
                    weigh(j, batches=GRANTED + c0 + BATCHES_PER_Q)
                for b in range(BATCHES_PER_Q, PRE_BATCHES):
                    if b + 1 < PRE_BATCHES:
                        one_hots(b + 1)
                    store_w(b)
                for first, last, build in ((0, BUILD_BODIES, True), (BUILD_BODIES, GROUPS - 1, False)):
                    with nc.vector.Fori(first, last) as i:
                        coefficients_lo(0, i)
                        if build:
                            batches = plus(GRANTED + c0 + PRE_BATCHES, i, BODY_BATCHES)
                        else:
                            batches = GRANTED + c0 + BATCHES
                        for j in range(GROUP_UNITS):
                            split_lo(base + GROUP + j + LEAD, i, GROUP_UNITS)
                            if build and j % 2 == 0:
                                one_hots(PRE_BATCHES + j // 2, i)
                            if j == 0:
                                dve.wait_ge(wa_lo, plus(layer * GROUPS + 1, i, 1))
                            if j < GROUP:
                                unit_done(dve, base + GROUP + j, i, GROUP_UNITS)
                                sum_halves(stage[:, j, :], a0 + GROUP + j)
                            if 1 <= j <= GROUP:
                                weigh(GROUP + j - 1, i, batches if j == 1 else None)
                            if j >= GROUP:
                                q = j - GROUP
                                if j == GROUP:
                                    dve.wait_ge(b_free, plus(GRANTED + b0, i, QUARTERS))
                                add_block(b0 + q, 512 * q, base + GROUP + j, i, GROUP_UNITS)
                            if build and j == 1:
                                dve.wait_ge(weighted, plus(layer * TILES + GROUP, i, GROUP))
                            if build and j % 2 == 1:
                                store_w(PRE_BATCHES + j // 2, i)
                coefficients_lo(GROUPS - 1)
                for q in range(QUARTERS):
                    split_lo(base + 2 * TILES - QUARTERS + q + LEAD)
                    add_block(b0 + QUARTERS * (GROUPS - 1) + q, 512 * q, base + 2 * TILES - QUARTERS + q)

            def routing(layer):
                w0, a0 = U0[f"wq{layer}"], A0[f"wq{layer}"]
                for u in range(2 * PEER_HEADS):
                    split_lo(w0 + u + LEAD)
                    if C0[f"wq{layer}"] + u - 1 > 0:
                        dve.wait_ge(c_full, C0[f"wq{layer}"] + u - 1)
                    unit_done(dve, w0 + u)
                    sum_halves(pq_t[:, u % 2, :], a0 + u)
                    if u >= 1:
                        route_unit(layer, u - 1)

            for s in (a_free, b_free, c_free):
                dve.sem_inc(s, GRANTED)
            dve.memset(eps_t[:], EPS).then_inc(dve_consts, 1)
            for m in range(LEAD):
                split_lo(m)
            scale_rows(0, lambda c: x_res[:, c, :], lambda c: xn[:, c, :], 0, xn_ready)
            dve.wait_ge(boot, 48)
            w = NC_TOK * HALF_ROPE
            pos_ff = soft[:, 0, 0:NC_TOK]
            steps.do(dve.tensor_copy(pos_ff, pos_i[:]))
            steps.sync()
            for c in range(NC_TOK):
                steps.do(dve.tensor_scalar(ang[:, 0, c * HALF_ROPE:(c + 1) * HALF_ROPE], invf[:],
                                           soft[:, 0, c:c + 1], None, ALU.mult))
            steps.sync()
            for shift, where in ((0.0, 4), (0.25, 5)):
                steps.do(dve.tensor_scalar(ang[:, 1, :], ang[:, 0, :], 1.0 / (2 * np.pi), shift, ALU.mult, ALU.add))
                steps.sync()
                steps.do(dve.tensor_scalar(ang[:, 1, :], ang[:, 1, :], ROUND, ROUND, ALU.add, ALU.subtract))
                steps.sync()
                src = ang[:, 0, :]
                for n, part in enumerate(TWO_PI_PARTS):
                    dst = ang[:, 2 + n % 2, :]
                    steps.do(dve.scalar_tensor_tensor(out=dst, in0=ang[:, 1, :], scalar=-part, in1=src,
                                                      op0=ALU.mult, op1=ALU.add))
                    steps.sync()
                    src = dst
                steps.do(dve.tensor_scalar(ang[:, where, :], src, 2 * np.pi * shift, None, ALU.add))
                steps.sync()
                steps.do(dve.tensor_scalar(ang[:, where, :], ang[:, where, :], PI_BELOW, -PI_BELOW, ALU.min, ALU.max))
                steps.sync()
            dve.sem_inc(angles, 1)
            gains_lo(A0["norm_sb"], KT, G_SB, act_t)

            dve.wait_ge(trig, 2)
            with nc.vector.Fori(0, 2 * HEADS // RAW_SLOTS) as i:
                for j in range(RAW_SLOTS):
                    split_lo(j + LEAD, i, RAW_SLOTS)
                    head = plus(j, i, RAW_SLOTS)
                    unit_done(dve, j, i, RAW_SLOTS)
                    dve.tensor_reduce(qk_t[:, bass.ds(head, 1), :].rearrange("p h t -> p (h t)"),
                                      ps_a[(A0["qk"] + j) % 2][:].rearrange("p (w t) -> p t w", w=2), AX.X,
                                      ALU.add).then_inc(a_free, 1)
            blocks(U0["v"], B0["v"], 4, lambda idx, col, last: copy_block(idx, v_tok, col, last))

            for h in range(HEADS + 2):
                if h < HEADS:
                    ps = ps_a[(A0["stick"] + h) % 2][:, 0:LIVE]
                    sp_, arg = st_sp[:, h % 2, :], st_arg[:, h % 2, :]
                    dve.wait_ge(a_full, AF0["stick"] + h + 1)
                    if h >= 2:
                        dve.wait_ge(st_exp, h - 1)
                    dve.tensor_scalar(arg, ps, SB_SCALE, None, ALU.mult).then_inc(a_free, 1)
                    dve.wait_ge(a_free, GRANTED + A0["stick"] + h + 1)
                    if h >= 2:
                        dve.wait_ge(st_masked, h - 1)
                    steps.do(dve.tensor_scalar(sp_, arg, 0.0, None, ALU.max))
                    steps.sync()
                    dve.wait_ge(st_log, h + 1)
                    dve.tensor_tensor(sp_, sp_, st_l[:, h % 2, :], ALU.add).then_inc(st_soft, 1)
                    dve.wait_ge(st_soft, h + 1)
                    steps.do(dve.tensor_tensor(arg, arg, sp_, ALU.subtract))
                if 1 <= h <= HEADS:
                    g = h - 1
                    arg = st_arg[:, g % 2, :]
                    dve.wait_ge(c_full, C0["stick"] + g + 1)
                    steps.sync()
                    dve.tensor_tensor(arg, arg, ps_c[(C0["stick"] + g) % 2][:, 0:LIVE],
                                      ALU.subtract).then_inc(st_args, 1)
                    dve.wait_ge(st_args, g + 1)
                    dve.sem_inc(c_free, 1)
                if h >= 2:
                    output_lo(h - 2, B0["stick"], 0)
            blocks(U0["wo"], B0["wo"], 4, add_block)

            def block_norm(k, a0, col):
                scale_rows(k, lambda c: x_res[:, c, :], lambda c: xn[:, c, :], 0, xn_ready)
                gains_lo(a0, KT, col, act_t)

            block_norm(1, A0["norm_p0"], G_P0)
            routing(0)
            peer(0)

            block_norm(2, A0["norm_kv"], G_KV)
            for n in range(U0["c"], U0["rope"] + 1):
                split_lo(n + LEAD)
            gains_lo(A0["norm_mla"], KT, G_MLA, act_t)
            c_idx, r_idx = B0["c"], B0["rope"]
            unit_done(dve, U0["c"] + 3)
            scale_rows(3, lambda c: ps_b[c_idx % 2][c][:], lambda c: c_tok[:, c, :], 4, xn_ready)
            dve.wait_ge(xn_ready, 4)
            dve.sem_inc(b_free, 1)
            unit_done(dve, U0["rope"])
            for c in range(NC_TOK):
                for twice in range(2):
                    rotate(ps_b[r_idx % 2][c][:, 0:ROPE].unsqueeze(1),
                           kr_tok[:, c, twice * ROPE:(twice + 1) * ROPE].unsqueeze(1), c, 1)
            dve.sem_inc(kr_ready, 1)
            dve.sem_inc(b_free, 1)
            gains_lo(A0["ct"], LT, G_LKV, c_t)
            dve.wait_ge(a_full, AF0["krt"] + 1)
            dve.tensor_copy(kr_t[:], ps_a[A0["krt"] % 2][:, 0:S]).then_inc(a_free, 1)
            for n in range(U0["dq"], U0["kn"]):
                split_lo(n + LEAD)
            d_idx = B0["dq"]
            unit_done(dve, U0["dq"] + 3)
            scale_rows(4, lambda c: ps_b[d_idx % 2][c][:], lambda c: c_tok[:, c, :], 8, xn_ready)
            dve.wait_ge(xn_ready, 5)
            dve.sem_inc(b_free, 1)

            def head_products(phase, dst):
                first = U0[phase]
                for n in range(HEADS // 4):
                    for j, s, k in halves(first + n, None, 0):
                        dve.wait_ge(a_full, AF0[phase] + 2 * n + j + 1)
                        sum_halves(dst[:, 4 * n + 2 * j, :], A0[phase] + 4 * n + 2 * j)
                        dve.wait_ge(used[s], k + 1)
                        sum_halves(dst[:, 4 * n + 2 * j + 1, :], A0[phase] + 4 * n + 2 * j + 1)
                    split_lo(first + n + LEAD)

            head_products("kn", kn_t)
            for nb in range(4):
                split_lo(U0["mv"] + nb + LEAD)
                copy_block(B0["mv"] + nb, mv_tok, 512 * nb, U0["mv"] + nb)
            gains_lo(A0["cqt"], LT, G_LQ, cq_t)
            head_products("uqn", qn_t)
            for nb in range(2):
                split_lo(U0["uqr"] + nb + LEAD)
                idx = B0["uqr"] + nb
                unit_done(dve, U0["uqr"] + nb)
                for c in range(NC_TOK):
                    rotate(ps_b[idx % 2][c][:].rearrange("p (h f) -> p h f", f=ROPE),
                           qr_tok[:, c, 512 * nb:512 * (nb + 1)].rearrange("p (h f) -> p h f", f=ROPE), c, 8)
                dve.sem_inc(b_free, 1)
            dve.sem_inc(qr_ready, 1)
            for f in range(4):
                idx = A0["qrt"] + f
                dve.wait_ge(a_full, AF0["qrt"] + f + 1)
                dve.tensor_copy(qr_t[:, 2 * f:2 * f + 2, :].rearrange("p h t -> p (h t)"),
                                ps_a[idx % 2][:]).then_inc(a_free, 1)
            for h in range(HEADS + 2):
                if h < HEADS:
                    idx = A0["mla"] + h
                    s_, m_ = ml_s[:, h % 2, :], ml_stat[:, h % 2, :]
                    dve.wait_ge(a_full, AF0["mla"] + h + 1)
                    if h >= 2:
                        dve.wait_ge(ml_exp, h - 1)
                    outer = s_.rearrange("p (b k) -> p b k", b=3)[:, 0:3:2, :]
                    outer_ps = ps_a[idx % 2][:, 0:LIVE].rearrange("p (b k) -> p b k", b=3)[:, 0:3:2, :]
                    steps.do(dve.tensor_tensor(outer, outer_ps, neg_upper[:].unsqueeze(1).to_broadcast([P, 2, P]),
                                               ALU.add))
                    dve.tensor_copy(s_[:, P:2 * P], ps_a[idx % 2][:, P:2 * P]).then_inc(a_free, 1)
                    steps.sync()
                    dve.wait_ge(a_free, GRANTED + idx + 1)
                    steps.do(dve.tensor_reduce(m_[:, 0:1], s_[:, 0:P], AX.X, ALU.max))
                    steps.do(dve.tensor_reduce(m_[:, 1:2], s_[:, P:LIVE], AX.X, ALU.max))
                    steps.sync()
                    dve.tensor_scalar(m_[:, 2:4], m_[:, 0:2], -MLA_SCALE, None, ALU.mult).then_inc(ml_masked, 1)
                if 1 <= h <= HEADS:
                    g = h - 1
                    m_ = ml_stat[:, g % 2, :]
                    dve.wait_ge(ml_exp, g + 1)
                    steps.do(dve.reciprocal(m_[:, 6:8], m_[:, 4:6]))
                    steps.sync()
                    for c, (lo_col, hi_col) in enumerate(((0, P), (P, LIVE))):
                        pr = ml_p[:, g % 2, lo_col:hi_col]
                        ins = dve.tensor_scalar(pr, pr, m_[:, 6 + c:7 + c], None, ALU.mult)
                    ins.then_inc(ml_norm, 1)
                if h >= 2:
                    output_lo(h - 2, B0["mla"], HEADS)
            blocks(U0["mwo"], B0["mwo"], 4, add_block)

            block_norm(5, A0["norm_p1"], G_P1)
            routing(1)
            peer(1)

            dve.wait_ge(stds, 7)
            steps.do(dve.reciprocal(stat[:, 2:4], stat[:, 0:2]))
            steps.sync()
            dve.wait_ge(gain_row_in, 16)
            for c in range(NC_TOK):
                dve.scalar_tensor_tensor(out=xn[:, c, :], in0=x_res[:, c, :], scalar=stat[:, 2 + c:3 + c],
                                         in1=gain_row[:], op0=ALU.mult, op1=ALU.mult).then_inc(final_ready, 1)

        @block.tensor
        def _(pe):
            mm = pe.matmul

            def weights_by_features(n0, ps, it=None, per=0, middle=None):
                for j, s, k in halves(n0, it, per):
                    pe.wait_ge(lo_ready[s], k + 1)
                    if j and middle:
                        middle()
                    for q in range(KT // 2):
                        kt = KT // 2 * j + q
                        w_hi, w_lo = (t[:, s, q * P:(q + 1) * P] for t in (hi, lo))
                        first, last = kt == 0, kt == KT - 1
                        if not first:
                            mm(ps[:, 0:S], w_lo, act_t[:, kt, 0, :], start=False, stop=False, skip_group_check=True)
                        ins = mm(ps[:], w_hi, act_t[:, kt, :, :].rearrange("p w t -> p (w t)"), start=first, stop=last)
                        if first:
                            ins = mm(ps[:, 0:S], w_lo, act_t[:, kt, 0, :], start=False, stop=False,
                                     skip_group_check=True)
                    ins.then_inc(used[s], 1)

            def unit_a(n0, idx, it=None, per=0, a_per=0, middle=None):
                pe.wait_ge(a_free, plus(idx + 1, it, a_per))
                weights_by_features(n0, ps_a[idx % 2], it, per, middle)

            def tokens_by_columns(n0, pair, act, kt0, kt_end, it=None, per=0, width=512, k_tiles=2):
                for j, s, k in halves(n0, it, per):
                    pe.wait_ge(lo_ready[s], k + 1)
                    for q in range(k_tiles):
                        kt = kt0 + k_tiles * j + q
                        w_hi, w_lo = (t[:, s, q * width:(q + 1) * width] for t in (hi, lo))
                        for c in range(NC_TOK):
                            a_hi, a_lo = (act[:, kt, w, c * P:(c + 1) * P] for w in range(2))
                            o = pair[c][:, 0:width]
                            mm(o, a_hi, w_hi, start=(kt == 0), stop=False)
                            mm(o, a_hi, w_lo, start=False, stop=False)
                            ins = mm(o, a_lo, w_hi, start=False, stop=(kt == kt_end - 1))
                    ins.then_inc(used[s], 1)

            def block_b(n0, idx, act, n_units, it=None, per=0, b_per=0):
                pe.wait_ge(b_free, plus(idx + 1, it, b_per))
                for u in range(n_units):
                    tokens_by_columns(n0 + u, ps_b[idx % 2], act, 4 * u, 4 * n_units, it, per)

            def turn(blocks_, a0):
                for f in range((len(blocks_) + 3) // 4):
                    idx = a0 + f
                    pe.wait_ge(a_free, idx + 1)
                    for q, blk in enumerate(blocks_[4 * f:4 * f + 4]):
                        ins = pe.transpose(ps_a[idx % 2][:, q * P:(q + 1) * P], blk, ident[:])
                    ins.then_inc(a_full, 1)

            def turn_rows(rows, k_tiles, a0):
                turn([rows[:, c, kt * P:(kt + 1) * P] for kt in range(k_tiles) for c in range(NC_TOK)], a0)

            def norm(count, a0):
                pe.wait_ge(xn_ready, count)
                turn_rows(xn, KT, a0)
                pe.wait_ge(a_free, GRANTED + a0 + KT // 2)

            def head_products(first, a0, act):
                for n in range(HEADS // 4):
                    for j, s, k in halves(first + n, None, 0):
                        pe.wait_ge(lo_ready[s], k + 1)
                        for m in range(2):
                            idx = a0 + 4 * n + 2 * j + m
                            pe.wait_ge(a_free, idx + 1)
                            ps = ps_a[idx % 2]
                            for kt in range(LT):
                                at = (LT * m + kt) * P
                                w_hi, w_lo = (t[:, s, at:at + P] for t in (hi, lo))
                                last = kt == LT - 1
                                if not last:
                                    mm(ps[:], w_hi, act[:, kt, :, :].rearrange("p w t -> p (w t)"), start=(kt == 0),
                                       stop=False, skip_group_check=True)
                                mm(ps[:, 0:S], w_lo, act[:, kt, 0, :], start=False, stop=False, skip_group_check=True)
                                if last:
                                    ins = mm(ps[:], w_hi, act[:, kt, :, :].rearrange("p w t -> p (w t)"), start=False,
                                             stop=True, skip_group_check=True)
                            ins.then_inc(a_full if m == 0 else used[s], 1)

            def head_outputs(idx, h, v, w):
                v0, v1 = (v[:, c, h * P:(h + 1) * P] for c in range(NC_TOK))
                ps = ps_b[idx % 2][0]
                mm(ps[:, 0:P], v0, w[:, 0:P], start=True, stop=True)
                mm(ps[:, P:S], v0, w[:, P:2 * P], start=True, stop=False)
                mm(ps[:, P:S], v1, w[:, 2 * P:LIVE], start=False, stop=True).then_inc(b_full, 1)

            def keys_product(layer, u):
                idx = C0[f"wq{layer}"] + u
                pe.wait_ge(a_free, GRANTED + A0[f"wq{layer}"] + u + 1)
                pe.wait_ge(keys_in, 16 * (layer + 1))
                pe.wait_ge(c_free, idx + 1)
                for c in range(NC_TOK):
                    ins = mm(ps_c[idx % 2][:, c * P:(c + 1) * P], pq_t[:, u % 2, c * P:(c + 1) * P], keys_sb[:, u, :],
                             start=True, stop=True)
                ins.then_inc(c_full, 1)

            def peer(layer):
                base = U0[f"peer{layer}"]
                a0, b0, c0 = A0[f"peer{layer}"], B0[f"peer{layer}"], C0[f"peer{layer}"]

                def build_w(b, it=None):
                    count = plus(layer * BATCHES + b + 1, it, BODY_BATCHES)
                    pe.wait_ge(c_free, plus(c0 + b + 1, it, BODY_BATCHES))
                    pe.wait_ge(hot2_ready, count)
                    pe.wait_ge(hot1g_ready, 2 * count)
                    for t in range(BATCH):
                        ins = mm(ps_c[(c0 + b) % 2][:, t * 2 * WQ_TILES:(t + 1) * 2 * WQ_TILES],
                                 hot2[:, b % 2, :, t], hot1g[:, b % 2, :, :, t].rearrange("p w i -> p (w i)"),
                                 start=True, stop=True)
                    ins.then_inc(c_full, 1)

                for j in range(GROUP):
                    unit_a(base + j, a0 + j,
                           middle=(lambda: keys_product(layer, 2 * PEER_HEADS - 1)) if j == 0 else None)
                pe.wait_ge(sel_ready, layer + 1)
                blocks_ = [sel_f[:, w, c, :] for w in range(3) for c in range(NC_TOK)]
                for f, some in enumerate((blocks_[0:4], blocks_[4:6])):
                    idx = C0[f"sel{layer}"] + f
                    pe.wait_ge(c_free, idx + 1)
                    for q, blk in enumerate(some):
                        ins = pe.transpose(ps_c[idx % 2][:, q * P:(q + 1) * P], blk, ident[:])
                    ins.then_inc(c_full, 1)
                with nc.tensor.Fori(0, PRE_BATCHES // BODY_BATCHES) as i:
                    for b in range(BODY_BATCHES):
                        build_w(b, i)
                for first, last, build in ((0, BUILD_BODIES, True), (BUILD_BODIES, GROUPS - 1, False)):
                    with nc.tensor.Fori(first, last) as i:
                        for j in range(GROUP_UNITS):
                            if j < GROUP:
                                unit_a(base + GROUP + j, a0 + GROUP + j, i, GROUP_UNITS, GROUP)
                            else:
                                if j == GROUP:
                                    pe.wait_ge(wa_lo, plus(layer * GROUPS + 1, i, 1))
                                block_b(base + GROUP + j, b0 + j - GROUP, wa, 1, i, GROUP_UNITS, QUARTERS)
                            if build and j % 2 == 1:
                                build_w(PRE_BATCHES + j // 2, i)
                pe.wait_ge(wa_lo, (layer + 1) * GROUPS)
                for q in range(QUARTERS):
                    block_b(base + 2 * TILES - QUARTERS + q, b0 + QUARTERS * (GROUPS - 1) + q, wa, 1)

            def routing(layer):
                for u in range(2 * PEER_HEADS):
                    unit_a(U0[f"wq{layer}"] + u, A0[f"wq{layer}"] + u,
                           middle=(lambda u=u: keys_product(layer, u - 1)) if u else None)

            pe.wait_ge(consts, N_CONSTS)
            norm(1, A0["norm_sb"])
            with nc.tensor.Fori(0, 2 * HEADS // RAW_SLOTS) as i:
                for j in range(RAW_SLOTS):
                    unit_a(j, A0["qk"] + j, i, RAW_SLOTS, RAW_SLOTS)
            for nb in range(4):
                block_b(U0["v"] + 4 * nb, B0["v"] + nb, act_t, 4)

            pe.wait_ge(a_free, GRANTED + A0["qk"] + 2 * HEADS)
            pe.wait_ge(b_free, GRANTED + B0["v"] + 4)
            for h in range(HEADS + 2):
                if h < HEADS:
                    idx = A0["stick"] + h
                    pe.wait_ge(a_free, idx + 1)
                    qh, kh = qk_t[:, h, :], qk_t[:, HEADS + h, :]
                    mm(ps_a[idx % 2][:, 0:S], kh[:, 0:P], qh, start=True, stop=True)
                    mm(ps_a[idx % 2][:, S:LIVE], kh[:, P:S], qh[:, P:S], start=True, stop=True).then_inc(a_full, 1)
                if 1 <= h <= HEADS:
                    g = h - 1
                    idx = C0["stick"] + g
                    ps, m = ps_c[idx % 2], st_spm[:, g % 2, :]
                    pe.wait_ge(c_free, idx + 1)
                    pe.wait_ge(st_masked, g + 1)
                    mm(ps[:, 0:P], tri[:], m[:, 0:P], start=True, stop=True)
                    mm(ps[:, P:2 * P], tri[:], m[:, P:2 * P], start=True, stop=False)
                    mm(ps[:, P:2 * P], ones[:], m[:, 2 * P:LIVE], start=False, stop=True)
                    mm(ps[:, 2 * P:LIVE], tri[:], m[:, 2 * P:LIVE], start=True, stop=True).then_inc(c_full, 1)
                if h >= 2:
                    g = h - 2
                    pe.wait_ge(b_free, B0["stick"] + g + 1)
                    pe.wait_ge(st_weights, g + 1)
                    head_outputs(B0["stick"] + g, g, v_tok, st_a[:, g % 2, :])
            pe.wait_ge(b_free, GRANTED + B0["stick"] + HEADS)
            for nb in range(4):
                block_b(U0["wo"] + 4 * nb, B0["wo"] + nb, act_t, 4)

            norm(2, A0["norm_p0"])
            routing(0)
            peer(0)

            norm(3, A0["norm_kv"])
            block_b(U0["c"], B0["c"], act_t, 4)
            pe.wait_ge(b_free, B0["rope"] + 1)
            n = U0["rope"]
            (_, s0, k0), (_, s1, k1) = halves(n, None, 0)
            pe.wait_ge(lo_ready[s0], k0 + 1)
            for kt in range(KT):
                w_hi, w_lo = (t[:, s0, kt * ROPE:(kt + 1) * ROPE] for t in (hi, lo))
                for c in range(NC_TOK):
                    a_hi, a_lo = (act_t[:, kt, w, c * P:(c + 1) * P] for w in range(2))
                    o = ps_b[B0["rope"] % 2][c][:, 0:ROPE]
                    mm(o, a_hi, w_hi, start=(kt == 0), stop=False)
                    mm(o, a_hi, w_lo, start=False, stop=False)
                    ins = mm(o, a_lo, w_hi, start=False, stop=(kt == KT - 1))
            ins.then_inc(used[s0], 1)
            pe.wait_ge(used[s0], k0 + 1)
            pe.wait_ge(lo_ready[s1], k1 + 1)
            pe.sem_inc(used[s1], 1)
            turn_rows(xn, KT, A0["norm_mla"])
            pe.wait_ge(xn_ready, 4)
            turn_rows(c_tok, LT, A0["ct"])
            pe.wait_ge(kr_ready, 1)
            turn([kr_tok[:, c, :] for c in range(NC_TOK)], A0["krt"])
            pe.wait_ge(a_free, GRANTED + A0["krt"] + 1)
            block_b(U0["dq"], B0["dq"], act_t, 4)
            head_products(U0["kn"], A0["kn"], c_t)
            for nb in range(4):
                block_b(U0["mv"] + nb, B0["mv"] + nb, c_t, 1)
            pe.wait_ge(xn_ready, 5)
            turn_rows(c_tok, LT, A0["cqt"])
            pe.wait_ge(a_free, GRANTED + A0["cqt"] + 2)
            head_products(U0["uqn"], A0["uqn"], cq_t)
            for nb in range(2):
                block_b(U0["uqr"] + nb, B0["uqr"] + nb, cq_t, 1)
            pe.wait_ge(qr_ready, 1)
            turn([qr_tok[:, c, h * P:(h + 1) * P] for h in range(HEADS // 2) for c in range(NC_TOK)], A0["qrt"])
            pe.wait_ge(a_free, GRANTED + A0["qrt"] + 4)
            pe.wait_ge(b_free, GRANTED + B0["mv"] + 4)
            for h in range(HEADS + 2):
                if h < HEADS:
                    idx = A0["mla"] + h
                    ps, r = ps_a[idx % 2], slice(ROPE * (h % 2), ROPE * (h % 2 + 1))
                    pe.wait_ge(a_free, idx + 1)
                    for o, q, keys_of in ((slice(0, P), slice(0, P), slice(0, P)),
                                          (slice(P, LIVE), slice(P, S), slice(0, S))):
                        mm(ps[:, o], qn_t[:, h, q], kn_t[:, h, keys_of], start=True, stop=False)
                        ins = mm(ps[:, o], qr_t[r, h // 2, q], kr_t[r, keys_of], start=False, stop=True)
                    ins.then_inc(a_full, 1)
                if 1 <= h <= HEADS:
                    g = h - 1
                    idx = C0["mla"] + g
                    pe.wait_ge(c_free, idx + 1)
                    pe.wait_ge(ml_norm, g + 1)
                    for b in range(3):
                        ins = pe.transpose(ps_c[idx % 2][:, b * P:(b + 1) * P], ml_p[:, g % 2, b * P:(b + 1) * P],
                                           ident[:])
                    ins.then_inc(c_full, 1)
                if h >= 2:
                    g = h - 2
                    pe.wait_ge(b_free, B0["mla"] + g + 1)
                    pe.wait_ge(c_free, GRANTED + C0["mla"] + g + 1)
                    head_outputs(B0["mla"] + g, g, mv_tok, ml_pt[:, g % 2, :])
            pe.wait_ge(b_free, GRANTED + B0["mla"] + HEADS)
            for nb in range(4):
                block_b(U0["mwo"] + 4 * nb, B0["mwo"] + nb, act_t, 4)

            norm(6, A0["norm_p1"])
            routing(1)
            peer(1)


def unit_features(w):
    k, n = w.shape
    return w.reshape(k // P, P, n // P, P).transpose(2, 1, 0, 3).reshape(n // P, P, UNIT)


def unit_columns(w):
    k, n = w.shape
    return w.reshape(k // (4 * P), 4, P, n // 512, 512).transpose(3, 0, 2, 1, 4).reshape(-1, P, UNIT)


def unit_heads(w):
    return w.reshape(LT, P, HEADS // 4, 4, P).transpose(2, 1, 3, 0, 4).reshape(HEADS // 4, P, UNIT)


def unit_experts(out, u, v):
    ut = u.reshape(TILES, P, KT, P).transpose(0, 3, 2, 1).reshape(GROUPS, GROUP, P, UNIT)
    vt = v.reshape(GROUPS, GROUP, P, QUARTERS, 512).transpose(0, 3, 2, 1, 4).reshape(GROUPS, QUARTERS, P, UNIT)
    out[0:GROUP] = ut[0]
    body = out[GROUP:GROUP + (GROUPS - 1) * GROUP_UNITS].reshape(GROUPS - 1, GROUP_UNITS, P, UNIT)
    body[:, 0:GROUP] = ut[1:]
    body[:, GROUP:] = vt[:-1]
    out[2 * TILES - QUARTERS:] = vt[-1]


def kernel(**inputs):
    import concourse.bacc as bacc
    from concourse.bass_utils import run_bass_kernel_spmd

    a = {k: np.asarray(v) for k, v in inputs.items()}
    qkv = a["sb_w_qkv"][0]
    ukv = a["mla_w_ukv"].reshape(LORA, HEADS, 2 * P)
    uq = a["mla_w_uq"][0].reshape(LORA, HEADS, P + ROPE)
    rope_unit = np.zeros((1, P, UNIT), np.float32)
    rope_unit[0, :, 0:KT * ROPE] = (a["mla_w_dkv"][:, LORA:].reshape(KT, P, ROPE).transpose(1, 0, 2)
                                    .reshape(P, KT * ROPE))
    parts = {
        "qk": unit_features(qkv[:, :2 * D]), "v": unit_columns(qkv[:, 2 * D:]), "wo": unit_columns(a["sb_w_o"][0]),
        "wq0": unit_features(a["peer_w_q"][0]), "c": unit_columns(a["mla_w_dkv"][:, :LORA]), "rope": rope_unit,
        "dq": unit_columns(a["mla_w_dq"][0]), "kn": unit_heads(ukv[:, :, :P]),
        "mv": unit_columns(ukv[:, :, P:].reshape(LORA, D)), "uqn": unit_heads(uq[:, :, :P]),
        "uqr": unit_columns(uq[:, :, P:].reshape(LORA, HEADS * ROPE)), "mwo": unit_columns(a["mla_w_o"][0]),
        "wq1": unit_features(a["peer_w_q"][1]),
    }
    stream = np.empty((N_UNITS, P, UNIT), np.float32)
    for name, count in PHASE_UNITS:
        dst = stream[U0[name]:U0[name] + count]
        if name in parts:
            dst[:] = parts[name]
        else:
            layer = int(name[-1])
            unit_experts(dst, a["peer_u"][layer], a["peer_v"][layer])
    keys = np.stack([a["peer_keys_1"], a["peer_keys_2"]], axis=2)
    keys = np.ascontiguousarray(keys.transpose(0, 4, 1, 2, 3).reshape(2, P, 2 * PEER_HEADS * NKEYS))
    gains = np.concatenate([g.reshape(-1, P) for g in (
        a["sb_norm_g"][0], a["peer_norm_g"][0], a["kv_norm_g"], a["mla_norm_g"][0], a["peer_norm_g"][1],
        a["mla_kv_latent_g"], a["mla_q_latent_g"][0])]).T
    arrays = {
        "x": a["x"][0], "positions": a["positions"].reshape(NC_TOK, P).T, "stream": stream, "keys": keys,
        "gains": gains, "final_g": a["final_norm_g"].reshape(1, D),
        "inv_freq": (np.float32(10000.0) ** (-np.arange(0, ROPE, 2, dtype=np.float32) / ROPE)).reshape(1, HALF_ROPE),
    }
    arrays = {f"in_{k}": np.ascontiguousarray(v) for k, v in arrays.items()}
    nc = bacc.Bacc("TRN2", target_bir_lowering=False, num_devices=1)
    aps = {k[3:]: nc.dram_tensor(k, v.shape, mybir.dt.from_np(v.dtype), kind="ExternalInput").ap()
           for k, v in arrays.items()}
    out = nc.dram_tensor("out", (S, D), F32, kind="ExternalOutput").ap()
    build_program(nc, out=out, **aps)
    result = run_bass_kernel_spmd(nc, [arrays], core_ids=[0])
    return result.results[0]["out"].reshape(1, S, D)
```

```python
from contextlib import ExitStack

import numpy as np
import concourse.bass as bass
from concourse import mybir

F32 = mybir.dt.float32
F32R = mybir.dt.float32r
U32 = mybir.dt.uint32
I32 = mybir.dt.int32
F16 = mybir.dt.float16
ALU = mybir.AluOpType
ACT = mybir.ActivationFunctionType
AX = mybir.AxisListType

P = 128
D = 2048
S = 256
NC_TOK = S // P
KT = D // P
HEADS = 16
LORA = 512
LT = LORA // P
ROPE = 64
HALF_ROPE = ROPE // 2
PEER_HEADS = 8
TOPK = 16
NKEYS = 128
EPS = 1e-6
UNIT = 2048
HALF = UNIT // 2
RAW_SLOTS = 4
HALF_SLOTS = 4
LEAD = 2
TILES = NKEYS
GROUP = 4
GROUPS = TILES // GROUP
QUARTERS = D // 512
GROUP_UNITS = GROUP + QUARTERS
WQ_TILES = 16
BATCH = 16
BATCHES_PER_Q = S // BATCH
BATCHES = BATCHES_PER_Q * (TILES // WQ_TILES)
BODY_BATCHES = 4
PRE_BATCHES = BATCHES_PER_Q + BODY_BATCHES
AHEAD = 5
AHEAD_TILES = AHEAD * GROUP
FULL_BODIES = GROUPS - AHEAD
assert PRE_BATCHES + FULL_BODIES * BODY_BATCHES == BATCHES
TURN_TILE = 7
BUILD_TILE = 8
TAIL = AHEAD_TILES + FULL_BODIES * GROUP_UNITS
EXP_TILE = 3


SB_SCALE = 128 ** -0.5
MLA_SCALE = (128 + ROPE) ** -0.5
NEG = -1e30
WEIGHT_SCALE = 2.0 ** 15
N_CONSTS = 11
TWO_PI_PARTS = (6.28125, 0.0019350051879882812, 3.0199159795074593e-07)
PI_BELOW = 3.1415925
ROUND = 1.5 * 2.0 ** 23

PHASE_UNITS = [("qk", 32), ("v", 16), ("wo", 16), ("wq0", 16), ("peer0", 2 * TILES),
               ("c", 4), ("rope", 1), ("dq", 4), ("kn", 4), ("mv", 4), ("uqn", 4), ("uqr", 2),
               ("mwo", 16), ("wq1", 16), ("peer1", 2 * TILES)]
PHASE_A = [("norm_sb", 8), ("qk", 32), ("stick", 16), ("norm_p0", 8), ("wq0", 16), ("peer0", TILES),
           ("norm_kv", 8), ("norm_mla", 8), ("ct", 2), ("krt", 1), ("kn", 16), ("cqt", 2), ("uqn", 16),
           ("qrt", 4), ("mla", 16), ("norm_p1", 8), ("wq1", 16), ("peer1", TILES)]
PHASE_B = [("v", 4), ("stick", 16), ("wo", 4), ("peer0", GROUPS * QUARTERS), ("c", 1), ("rope", 1),
           ("dq", 1), ("mv", 4), ("uqr", 2), ("mla", 16), ("mwo", 4), ("peer1", GROUPS * QUARTERS)]
PHASE_C = [("stick", 16), ("wq0", 16), ("sel0", 2), ("peer0", BATCHES), ("mla", 16), ("wq1", 16),
           ("sel1", 2), ("peer1", BATCHES)]


def starts(table):
    out, n = {}, 0
    for name, count in table:
        out[name] = n
        n += count
    return out, n


U0, N_UNITS = starts(PHASE_UNITS)
A0, _ = starts(PHASE_A)
B0, _ = starts(PHASE_B)
C0, _ = starts(PHASE_C)
AF0, _ = starts([("norm_sb", 8), ("stick", 16), ("norm_p0", 8), ("norm_kv", 8), ("norm_mla", 8), ("ct", 2),
                 ("krt", 1), ("kn", 8), ("cqt", 2), ("uqn", 8), ("qrt", 4), ("mla", 16), ("norm_p1", 8)])
BF0, _ = starts([("stick", 16), ("mla", 16)])

G_SB, G_P0, G_KV, G_MLA, G_P1 = (KT * i for i in range(5))
G_LKV = 5 * KT
G_LQ = G_LKV + LT
N_GAINS = G_LQ + LT


def batch_at(tile, half):
    h, places = 2 * (tile - BUILD_TILE) + half, 2 * (AHEAD_TILES - BUILD_TILE)
    b = -(-h * PRE_BATCHES // places)
    return b if h >= 0 and b < PRE_BATCHES and b * places // PRE_BATCHES == h else None


def plus(base, it, step):
    return base if it is None else it * step + base


class Steps:

    def __init__(self, engine, semaphore):
        self.engine, self.semaphore, self.count = engine, semaphore, 0

    def do(self, instruction):
        instruction.then_inc(self.semaphore, 1)
        self.count += 1

    def sync(self):
        self.engine.wait_ge(self.semaphore, self.count)


def build_program(nc, x, positions, stream, keys, gains, final_g, inv_freq, out):
    with ExitStack() as ctx:
        def sem(name):
            return ctx.enter_context(nc.semaphore(name))

        def sb(name, shape, dt=F32):
            return ctx.enter_context(nc.sbuf_tensor(name, shape, dt))

        x_res = sb("x_res", [P, NC_TOK, D])
        act_t = sb("act_t", [P, KT, 2, S], F32R)
        raw = sb("raw", [P, RAW_SLOTS, UNIT])
        hi = sb("hi", [P, HALF_SLOTS, HALF], F32R)
        lo = sb("lo", [P, HALF_SLOTS, HALF], F32R)
        ident = sb("ident", [P, P])
        iota = sb("iota", [P, P])
        neg_upper = sb("neg_upper", [P, P])
        gain_t = sb("gain_t", [P, N_GAINS])
        eps_t = sb("eps_t", [P, 1])
        stat = sb("stat", [P, 16])
        cos_t = sb("cos_t", [P, NC_TOK, HALF_ROPE])
        sin_t = sb("sin_t", [P, NC_TOK, HALF_ROPE])

        KB = 1024
        arena_kb = 93
        arena_at = (nc.sbuf_base + 31) // 32 * 32
        sb("arena", [P, arena_kb * KB // 4])

        def place(name, kb, shape, dt=F32):
            size = 4 * int(np.prod(shape[1:]))
            assert kb * KB + size <= arena_kb * KB, name
            return nc.alloc_sbuf_tensor_at(name, shape, dt, offset=arena_at + int(kb * KB))

        xn = place("xn", 72, [P, NC_TOK, D])
        qk_t = place("qk_t", 0, [P, 2 * HEADS, S])
        v_tok = place("v_tok", 32, [P, NC_TOK, D])
        tri = place("tri", 48, [P, P])
        ones = place("ones", 48.5, [P, P])
        below = place("below", 49, [P, 3, P])
        LIVE = 3 * P
        st_l = place("st_l", 51, [P, 2, LIVE])
        st_sp = place("st_sp", 54, [P, 2, LIVE])
        st_spm = place("st_spm", 57, [P, 2, LIVE])
        st_arg = place("st_arg", 60, [P, 2, LIVE])
        st_e = place("st_e", 63, [P, 2, LIVE])
        st_a = place("st_a", 66, [P, 2, LIVE])
        qn_t = place("qn_t", 0, [P, HEADS, S])
        kn_t = place("kn_t", 16, [P, HEADS, S])
        mv_tok = place("mv_tok", 32, [P, NC_TOK, D])
        qr_t = place("qr_t", 48, [P, HEADS // 2, S])
        c_t = place("c_t", 56, [P, LT, 2, S], F32R)
        cq_t = place("cq_t", 64, [P, LT, 2, S], F32R)
        qr_tok = place("qr_tok", 72, [P, NC_TOK, HEADS * ROPE])
        rope_u = place("rope_u", 80, [P, 8 * HALF_ROPE])
        rope_v = place("rope_v", 81, [P, 8 * HALF_ROPE])
        c_tok = place("c_tok", 88, [P, NC_TOK, LORA])
        kr_tok = place("kr_tok", 92, [P, NC_TOK, 2 * ROPE])
        kr_t = place("kr_t", 92, [P, S])
        ml_s = place("ml_s", 72, [P, 2, LIVE])
        ml_p = place("ml_p", 75, [P, 2, LIVE])
        ml_pt = place("ml_pt", 78, [P, 2, LIVE])
        ml_stat = place("ml_stat", 81, [P, 2, 8])
        keys_sb = place("keys_sb", 0, [P, 2 * PEER_HEADS, NKEYS])
        pq_t = place("pq_t", 8, [P, 2, S])
        top_v = place("top_v", 10, [P, NC_TOK, PEER_HEADS, 2, TOPK])
        top_i = place("top_i", 12, [P, NC_TOK, PEER_HEADS, 2, TOPK], U32)
        top_f = place("top_f", 14, [P, NC_TOK, PEER_HEADS, 2, TOPK])
        cut = place("cut", 16, [P, NC_TOK, NKEYS])
        cand = place("cand", 17, [P, NC_TOK, TOPK * TOPK])
        cand_cut = place("cand_cut", 19, [P, NC_TOK, TOPK * TOPK])
        sel_v = place("sel_v", 21, [P, NC_TOK, PEER_HEADS, TOPK])
        sel_p = place("sel_p", 22, [P, NC_TOK, PEER_HEADS, TOPK], U32)
        pos_u = place("pos_u", 23, [P, 2, NC_TOK * P], U32)
        pos_f = place("pos_f", 25, [P, 2, NC_TOK * P])
        sel_f = place("sel_f", 27, [P, 3, NC_TOK, P])
        soft = place("soft", 30, [P, 4, NC_TOK * PEER_HEADS])
        match = place("match", 32, [P, TOPK, NC_TOK * P])
        w_route = place("w_route", 0, [P, 2 * WQ_TILES, S])
        was = [place(f"wa{i}", 32 + 8 * i, [P, GROUP, 2, S], F32R) for i in range(2)]
        wa = was[0]
        stage = place("stage", 48, [P, AHEAD_TILES, S])
        iota_rep = place("iota_rep", 68, [P, P, BATCH], F16)
        hot2 = place("hot2", 72, [P, 2, P, BATCH], F16)
        hot1 = place("hot1", 80, [P, WQ_TILES, BATCH], F16)
        hot1g = place("hot1g", 80.5, [P, 2, 2, WQ_TILES, BATCH], F16)
        i1_t = place("i1_t", 82.5, [P, S], F16)
        i2_t = place("i2_t", 83, [P, S], F16)
        g_parts = place("g_parts", 83.5, [P, 2, S], F16)
        g_full = place("g_full", 84.5, [P, S])
        gain_row = place("gain_row", 0, [P, D])
        pos_i = place("pos_i", 0, [P, NC_TOK], I32)
        ang = place("ang", 1, [P, 6, NC_TOK * HALF_ROPE])
        invf = place("invf", 4, [P, HALF_ROPE])

        bank = [ctx.enter_context(nc.psum_tensor(f"bank{i}", [P, 512], F32)) for i in range(8)]
        ps_a = bank[0:2]
        ps_b = [bank[2:4], bank[4:6]]
        ps_c = bank[6:8]

        boot = sem("boot")
        x_in = sem("x_in")
        consts = sem("consts")
        raw_in = [sem(f"raw_in{i}") for i in range(RAW_SLOTS)]
        hi_ready = [sem(f"hi_ready{i}") for i in range(HALF_SLOTS)]
        lo_ready = [sem(f"lo_ready{i}") for i in range(HALF_SLOTS)]
        used = [sem(f"used{i}") for i in range(HALF_SLOTS)]
        a_full, a_free = sem("a_full"), sem("a_free")
        b_full, b_free = sem("b_full"), sem("b_free")
        c_full, c_free = sem("c_full"), sem("c_free")
        dve_step = sem("dve_step")
        act_step = sem("act_step")
        stds = sem("stds")
        xn_ready = sem("xn_ready")
        gain_hi = sem("gain_hi")
        angles = sem("angles")
        trig = sem("trig")
        st_log = sem("st_log")
        st_soft = sem("st_soft")
        st_masked = sem("st_masked")
        st_args = sem("st_args")
        st_exp = sem("st_exp")
        st_weights = sem("st_weights")
        ot_hi = sem("ot_hi")
        kr_ready = sem("kr_ready")
        qr_ready = sem("qr_ready")
        ml_masked = sem("ml_masked")
        ml_exp = sem("ml_exp")
        ml_norm = sem("ml_norm")
        keys_in = sem("keys_in")
        soft_in = sem("soft_in")
        soft_out = sem("soft_out")
        sel_ready = sem("sel_ready")
        sel_t_ready = sem("sel_t_ready")
        hot1_ready = sem("hot1_ready")
        hots_ready = sem("hots_ready")
        gelu_done = sem("gelu_done")
        weighted = sem("weighted")
        wa_hi = sem("wa_hi")
        wa_lo = sem("wa_lo")
        final_ready = sem("final_ready")
        gain_row_in = sem("gain_row_in")
        stored = sem("stored")

        dve_consts = sem("dve_consts")
        GRANTED = 2

        def halves(n0, it, per):
            for j in range(2):
                h = 2 * n0 + j
                yield j, h % HALF_SLOTS, plus(h // HALF_SLOTS, it, 2 * per // HALF_SLOTS)

        def gpsimd_takes(n0, s):
            busy = any(U0[f"wq{k}"] + LEAD <= n0 < U0[f"peer{k}"] + AHEAD_TILES + LEAD for k in range(2))
            return s >= 1 if busy else s == HALF_SLOTS - 1

        def tail_wa(g):
            return was[(g - FULL_BODIES + 1) % 2]

        def unit_done(engine, n0, it=None, per=0):
            *_, (_, s, k) = halves(n0, it, per)
            engine.wait_ge(used[s], k + 1)

        block = ctx.enter_context(nc.Block())

        @block.sync
        def _(sp):
            sp.dma_start(gain_t[:], gains).then_inc(boot, 16)
            for c in range(NC_TOK):
                sp.dma_start(x_res[:, c, :], x[c * P:(c + 1) * P, :]).then_inc(x_in, 16)
            sp.dma_start(pos_i[:], positions).then_inc(boot, 16)
            sp.dma_start(invf[:], inv_freq.to_broadcast([P, HALF_ROPE])).then_inc(boot, 16)

            def load(n0, it=None, first=False):
                if not first:
                    for j, s, k in halves(n0 - RAW_SLOTS, it, RAW_SLOTS):
                        sp.wait_ge(lo_ready[s], k + 1)
                slot = n0 % RAW_SLOTS
                sp.dma_start(raw[:, slot, :], stream[plus(n0, it, RAW_SLOTS)]).then_inc(raw_in[slot], 16)

            for n in range(RAW_SLOTS):
                load(n, first=True)
            rounds = N_UNITS // RAW_SLOTS
            with nc.sync.Fori(0, rounds - 1) as i:
                for n in range(RAW_SLOTS):
                    load(RAW_SLOTS + n, i)
            for n in range(rounds * RAW_SLOTS, N_UNITS):
                load(n)
            for c in range(NC_TOK):
                sp.wait_ge(final_ready, c + 1)
                sp.dma_start(out[c * P:(c + 1) * P, :], xn[:, c, :]).then_inc(stored, 16)
            sp.wait_ge(stored, 16 * NC_TOK)

        @block.gpsimd
        def _(pool):
            pool.memset(ident[:], 0.0).then_inc(consts, 1)
            pool.memset(neg_upper[:], 0.0).then_inc(consts, 1)
            pool.memset(tri[:], 1.0).then_inc(consts, 1)
            pool.memset(ones[:], 1.0).then_inc(consts, 1)
            pool.memset(below[:], 1.0).then_inc(consts, 1)
            pool.wait_ge(consts, 5)
            pool.affine_select(out=ident[:], in_=ident[:], compare_op=ALU.not_equal, fill=1.0, base=0,
                               pattern=[[-1, P]], channel_multiplier=1).then_inc(consts, 1)
            pool.affine_select(out=neg_upper[:], in_=neg_upper[:], compare_op=ALU.is_ge, fill=NEG, base=0,
                               pattern=[[-1, P]], channel_multiplier=1).then_inc(consts, 1)
            pool.affine_select(out=tri[:], in_=tri[:], compare_op=ALU.is_gt, fill=0.0, base=0,
                               pattern=[[-1, P]], channel_multiplier=1).then_inc(consts, 1)
            for b in (0, 2):
                pool.affine_select(out=below[:, b, :], in_=below[:, b, :], compare_op=ALU.is_gt, fill=0.0,
                                   base=0, pattern=[[1, P]], channel_multiplier=-1).then_inc(consts, 1)
            pool.iota(iota[:], pattern=[[1, P]], base=0, channel_multiplier=0,
                      allow_small_or_imprecise_dtypes=True).then_inc(consts, 1)

            def split_lo(n0, it=None, per=0):
                for j, s, k in halves(n0, it, per):
                    if gpsimd_takes(n0, s) and n0 < N_UNITS:
                        pool.wait_ge(hi_ready[s], k + 1)
                        pool.tensor_tensor(lo[:, s, :], raw[:, n0 % RAW_SLOTS, j * HALF:(j + 1) * HALF],
                                           hi[:, s, :].bitcast(F32), ALU.subtract).then_inc(lo_ready[s], 1)

            def split_range(first, last):
                n = first
                rounds = (last - first) // RAW_SLOTS
                if rounds > 1:
                    with nc.gpsimd.Fori(0, rounds) as i:
                        for j in range(RAW_SLOTS):
                            split_lo(n + j, i, RAW_SLOTS)
                    n += rounds * RAW_SLOTS
                for m in range(n, last):
                    split_lo(m)

            def mask_head(h, src, dst, ready, freed, done):
                pool.wait_ge(ready, h + 1)
                if freed is not None and h >= 2:
                    pool.wait_ge(freed[0], freed[1] + h - 1)
                pool.tensor_tensor(dst[:, h % 2, :], src[:, h % 2, :],
                                   below[:].rearrange("p b q -> p (b q)"), ALU.mult).then_inc(done, 1)

            def peer(layer):
                base = U0[f"peer{layer}"]
                for j in range(AHEAD_TILES):
                    split_lo(base + j + LEAD)
                with nc.gpsimd.Fori(0, FULL_BODIES) as i:
                    for j in range(GROUP_UNITS):
                        split_lo(base + AHEAD_TILES + j + LEAD, i, GROUP_UNITS)
                split_range(base + TAIL + LEAD, min(base + 2 * TILES + LEAD, N_UNITS))

            split_range(0, U0["wo"] + LEAD)
            for h in range(HEADS + 1):
                if h < HEADS:
                    mask_head(h, st_sp, st_spm, st_soft, (c_full, C0["stick"]), st_masked)
                if h >= 1:
                    mask_head(h - 1, st_e, st_a, st_exp, (b_full, BF0["stick"]), st_weights)
            split_range(U0["wo"] + LEAD, U0["wq0"] + LEAD)
            split_range(U0["wq0"] + LEAD, U0["peer0"] + LEAD)
            peer(0)
            split_range(U0["c"] + LEAD, U0["wq1"] + LEAD)
            split_range(U0["wq1"] + LEAD, U0["peer1"] + LEAD)
            peer(1)

        @block.scalar
        def _(act):
            steps = Steps(act, act_step)

            def split_hi(n0, it=None, per=0):
                if n0 >= N_UNITS:
                    return
                slot = n0 % RAW_SLOTS
                act.wait_ge(raw_in[slot], plus(16 * (n0 // RAW_SLOTS + 1), it, 16 * per // RAW_SLOTS))
                for j, s, k in halves(n0, it, per):
                    if it is not None or k > 0:
                        act.wait_ge(used[s], k)
                    act.activation(hi[:, s, :], raw[:, slot, j * HALF:(j + 1) * HALF],
                                   ACT.Copy).then_inc(hi_ready[s], 1)

            def split_range(first, last):
                n = first
                rounds = (last - first) // RAW_SLOTS
                if rounds > 1:
                    with nc.scalar.Fori(0, rounds) as i:
                        for j in range(RAW_SLOTS):
                            split_hi(n + j, i, RAW_SLOTS)
                    n += rounds * RAW_SLOTS
                for m in range(n, last):
                    split_hi(m)

            def root_mean_square(k, rows, junk, width, col):
                for c in range(NC_TOK):
                    steps.do(act.activation(junk(c), rows(c), ACT.Square, accum_out=stat[:, col + c:col + c + 1]))
                steps.sync()
                act.activation(stat[:, col:col + NC_TOK], stat[:, col:col + NC_TOK], ACT.Sqrt,
                               bias=eps_t[:, 0:1], scale=1.0 / width).then_inc(stds, 1)

            def gains_hi(phase, k_tiles, col, dst):
                a0 = A0[phase]
                for f in range(k_tiles // 2):
                    act.wait_ge(a_full, AF0[phase] + f + 1)
                    for k in range(2):
                        kt = 2 * f + k
                        ins = act.activation(dst[:, kt, 0, :], ps_a[(a0 + f) % 2][:, k * S:(k + 1) * S], ACT.Copy,
                                             scale=gain_t[:, col + kt:col + kt + 1])
                    ins.then_inc(gain_hi, 1)

            def x_norm(k, b_end, phase, col):
                if b_end:
                    act.wait_ge(b_free, GRANTED + b_end)
                else:
                    act.wait_ge(x_in, 16 * NC_TOK)
                root_mean_square(k, lambda c: x_res[:, c, :], lambda c: xn[:, c, :], D, 0)
                gains_hi(phase, KT, col, act_t)

            def output_hi(h, phase):
                b0 = B0[phase]
                act.wait_ge(b_full, BF0[phase] + h + 1)
                act.activation(act_t[:, h, 0, :], ps_b[(b0 + h) % 2][0][:, 0:S], ACT.Copy).then_inc(ot_hi, 1)

            def peer(layer):
                base = U0[f"peer{layer}"]
                a0 = A0[f"peer{layer}"]

                def gelu(t, it=None):
                    act.wait_ge(a_free, plus(GRANTED + a0 + t + 1, it, GROUP))
                    st = stage[:, bass.ds(plus(t, it, GROUP) % AHEAD_TILES, 1), :]
                    act.activation(st, st, ACT.Gelu).then_inc(gelu_done, 1)

                def coefficients_hi(g, free, it=None, to=wa):
                    act.wait_ge(weighted, plus(layer * TILES + GROUP * (g + 1), it, GROUP))
                    unit_done(act, free, it, GROUP_UNITS)
                    first = plus(g * GROUP, it, GROUP) % AHEAD_TILES
                    act.activation(to[:, :, 0, :], stage[:, bass.ds(first, GROUP), :], ACT.Copy).then_inc(wa_hi, 1)

                act.preload_act_table_set("gelu_and_others")
                for j in range(AHEAD_TILES):
                    split_hi(base + j + LEAD)
                    gelu(j)
                    if j == EXP_TILE:
                        act.wait_ge(soft_in, layer + 1)
                        act.activation(sel_f[:, 2, :, :], sel_f[:, 2, :, :], ACT.Exp).then_inc(soft_out, 1)
                        act.preload_act_table_set("gelu_and_others")
                with nc.scalar.Fori(0, FULL_BODIES) as i:
                    coefficients_hi(0, base + AHEAD_TILES - 1, i)
                    for j in range(GROUP_UNITS):
                        split_hi(base + AHEAD_TILES + j + LEAD, i, GROUP_UNITS)
                        if j < GROUP:
                            gelu(AHEAD_TILES + j, i)
                for g in range(FULL_BODIES, GROUPS):
                    first = base + TAIL + QUARTERS * (g - FULL_BODIES)
                    if g == FULL_BODIES:
                        coefficients_hi(g, base + TAIL - 1 - GROUP_UNITS, to=tail_wa(g))
                    for j in range(QUARTERS):
                        split_hi(first + j + LEAD)
                        if j == 1 and g + 1 < GROUPS:
                            coefficients_hi(g + 1, first - 1, to=tail_wa(g + 1))

            def routing(layer):
                act.dma_start(keys_sb[:], keys[layer]).then_inc(keys_in, 16)
                split_range(U0[f"wq{layer}"] + LEAD, U0[f"peer{layer}"] + LEAD)

            act.wait_ge(boot, 48)
            act.wait_ge(dve_consts, 1)
            for m in range(LEAD):
                split_hi(m)
            x_norm(0, 0, "norm_sb", G_SB)
            act.wait_ge(angles, 1)
            act.activation(sin_t[:].rearrange("p c f -> p (c f)"), ang[:, 4, :], ACT.Sin).then_inc(trig, 1)
            act.activation(cos_t[:].rearrange("p c f -> p (c f)"), ang[:, 5, :], ACT.Sin).then_inc(trig, 1)
            split_range(LEAD, U0["wo"] + LEAD)

            act.preload_act_table_set("natural_log_exp_and_others")
            for h in range(HEADS + 2):
                if h < HEADS:
                    tmp = st_l[:, h % 2, :]
                    act.wait_ge(a_free, GRANTED + A0["stick"] + h + 1)
                    if h >= 2:
                        act.wait_ge(st_soft, h - 1)
                    steps.do(act.activation(tmp, st_arg[:, h % 2, :], ACT.Abs))
                    steps.sync()
                    steps.do(act.activation(tmp, tmp, ACT.Exp, scale=-1.0))
                    steps.sync()
                    act.activation(tmp, tmp, ACT.Ln, bias=1.0).then_inc(st_log, 1)
                if 1 <= h <= HEADS:
                    g = h - 1
                    act.wait_ge(st_args, g + 1)
                    if g >= 2:
                        act.wait_ge(st_weights, g - 1)
                    act.activation(st_e[:, g % 2, :], st_arg[:, g % 2, :], ACT.Exp).then_inc(st_exp, 1)
                if h >= 2:
                    output_hi(h - 2, "stick")
            split_range(U0["wo"] + LEAD, U0["wq0"] + LEAD)

            x_norm(1, B0["wo"] + 4, "norm_p0", G_P0)
            routing(0)
            peer(0)

            x_norm(2, B0["peer0"] + GROUPS * QUARTERS, "norm_kv", G_KV)
            split_range(U0["c"] + LEAD, U0["rope"] + 1 + LEAD)
            unit_done(act, U0["rope"])
            gains_hi("norm_mla", KT, G_MLA, act_t)
            unit_done(act, U0["c"] + 3)
            root_mean_square(3, lambda c: ps_b[B0["c"] % 2][c][:], lambda c: c_tok[:, c, :], LORA, 4)
            gains_hi("ct", LT, G_LKV, c_t)
            split_range(U0["dq"] + LEAD, U0["kn"] + LEAD)
            unit_done(act, U0["dq"] + 3)
            act.wait_ge(a_full, AF0["ct"] + 2)
            root_mean_square(4, lambda c: ps_b[B0["dq"] % 2][c][:], lambda c: c_tok[:, c, :], LORA, 8)
            split_range(U0["kn"] + LEAD, U0["uqn"] + LEAD)
            gains_hi("cqt", LT, G_LQ, cq_t)
            split_range(U0["uqn"] + LEAD, U0["mwo"] + LEAD)
            act.preload_act_table_set("exp_and_others")
            for h in range(HEADS + 2):
                if h < HEADS:
                    act.wait_ge(ml_masked, h + 1)
                    if h >= 2:
                        act.wait_ge(c_full, C0["mla"] + h - 1)
                    for c, (lo_col, hi_col) in enumerate(((0, P), (P, LIVE))):
                        ins = act.activation(ml_p[:, h % 2, lo_col:hi_col], ml_s[:, h % 2, lo_col:hi_col], ACT.Exp,
                                             bias=ml_stat[:, h % 2, 2 + c:3 + c], scale=MLA_SCALE,
                                             accum_out=ml_stat[:, h % 2, 4 + c:5 + c])
                    ins.then_inc(ml_exp, 1)
                if 1 <= h <= HEADS:
                    g = h - 1
                    act.wait_ge(c_full, C0["mla"] + g + 1)
                    if g >= 2:
                        act.wait_ge(b_full, BF0["mla"] + g - 1)
                    act.activation(ml_pt[:, g % 2, :], ps_c[(C0["mla"] + g) % 2][:, 0:LIVE],
                                   ACT.Copy).then_inc(c_free, 1)
                if h >= 2:
                    output_hi(h - 2, "mla")
            split_range(U0["mwo"] + LEAD, U0["wq1"] + LEAD)

            x_norm(5, B0["mwo"] + 4, "norm_p1", G_P1)
            routing(1)
            peer(1)

            act.wait_ge(b_free, GRANTED + B0["peer1"] + GROUPS * QUARTERS)
            act.dma_start(gain_row[:], final_g.to_broadcast([P, D])).then_inc(gain_row_in, 16)
            root_mean_square(6, lambda c: x_res[:, c, :], lambda c: xn[:, c, :], D, 0)

        @block.vector
        def _(dve):
            steps = Steps(dve, dve_step)

            def split_lo(n0, it=None, per=0):
                for j, s, k in halves(n0, it, per):
                    if not gpsimd_takes(n0, s) and n0 < N_UNITS:
                        dve.wait_ge(hi_ready[s], k + 1)
                        dve.tensor_tensor(lo[:, s, :], raw[:, n0 % RAW_SLOTS, j * HALF:(j + 1) * HALF],
                                          hi[:, s, :].bitcast(F32), ALU.subtract).then_inc(lo_ready[s], 1)

            def sum_halves(dst, idx):
                dve.tensor_reduce(dst, ps_a[idx % 2][:].rearrange("p (w t) -> p t w", w=2), AX.X,
                                  ALU.add).then_inc(a_free, 1)

            def scale_rows(k, rows, dst, col, done):
                dve.wait_ge(stds, k + 1)
                inv = stat[:, col + 2:col + 2 + NC_TOK]
                steps.do(dve.reciprocal(inv, stat[:, col:col + NC_TOK]))
                steps.sync()
                for c in range(NC_TOK):
                    ins = dve.tensor_scalar(dst(c), rows(c), stat[:, col + 2 + c:col + 3 + c], None, ALU.mult)
                    if c == NC_TOK - 1 and done is not None:
                        ins.then_inc(done, 1)

            gain_count = [0]

            def gains_lo(a0, k_tiles, col, dst):
                for f in range(k_tiles // 2):
                    gain_count[0] += 1
                    dve.wait_ge(gain_hi, gain_count[0])
                    for k in range(2):
                        kt = 2 * f + k
                        ins = dve.scalar_tensor_tensor(
                            out=dst[:, kt, 1, :], in0=ps_a[(a0 + f) % 2][:, k * S:(k + 1) * S],
                            scalar=gain_t[:, col + kt:col + kt + 1], in1=dst[:, kt, 0, :].bitcast(F32),
                            op0=ALU.mult, op1=ALU.subtract)
                    ins.then_inc(a_free, 1)

            def copy_block(idx, dst, col, last):
                unit_done(dve, last)
                for c in range(NC_TOK):
                    ins = dve.tensor_copy(dst[:, c, col:col + 512], ps_b[idx % 2][c][:])
                ins.then_inc(b_free, 1)

            def add_block(idx, col, last, it=None, per=0):
                unit_done(dve, last, it, per)
                for c in range(NC_TOK):
                    r = x_res[:, c, col:col + 512]
                    ins = dve.tensor_tensor(r, r, ps_b[idx % 2][c][:], ALU.add)
                ins.then_inc(b_free, 1)

            def output_lo(h, b0, count):
                dve.wait_ge(ot_hi, count + h + 1)
                dve.tensor_tensor(act_t[:, h, 1, :], ps_b[(b0 + h) % 2][0][:, 0:S],
                                  act_t[:, h, 0, :].bitcast(F32), ALU.subtract).then_inc(b_free, 1)

            def blocks(first, b0, n_blocks, store):
                for nb in range(n_blocks):
                    for j in range(4):
                        split_lo(first + 4 * nb + j + LEAD)
                    store(b0 + nb, 512 * nb, first + 4 * nb + 3)

            def rotate(src, dst, c, heads):
                def table(t):
                    return t[:, c, :].unsqueeze(1).to_broadcast([P, heads, HALF_ROPE])
                u = rope_u[:, 0:heads * HALF_ROPE].rearrange("p (h f) -> p h f", h=heads)
                v = rope_v[:, 0:heads * HALF_ROPE].rearrange("p (h f) -> p h f", h=heads)
                one, two = src[:, :, 0:HALF_ROPE], src[:, :, HALF_ROPE:ROPE]
                for x_, y_, where, op in ((one, two, 0, ALU.subtract), (two, one, HALF_ROPE, ALU.add)):
                    steps.do(dve.tensor_tensor(u, x_, table(cos_t), ALU.mult))
                    steps.do(dve.tensor_tensor(v, y_, table(sin_t), ALU.mult))
                    steps.sync()
                    steps.do(dve.tensor_tensor(dst[:, :, where:where + HALF_ROPE], u, v, op))
                    steps.sync()

            def top16(src, values, indices, cut_at, released=None):
                for c in range(NC_TOK):
                    steps.do(dve.max(values(c)[:, 0:8], src(c)))
                steps.sync()
                for c in range(NC_TOK):
                    steps.do(dve.match_replace(cut_at(c), values(c)[:, 0:8], src(c), -3e38))
                for c in range(NC_TOK):
                    ins = dve.max_index(indices(c)[:, 0:8], values(c)[:, 0:8], src(c))
                    if c == NC_TOK - 1 and released is not None:
                        ins.then_inc(released, 1)
                    else:
                        steps.do(ins)
                steps.sync()
                for c in range(NC_TOK):
                    steps.do(dve.max(values(c)[:, 8:16], cut_at(c)))
                steps.sync()
                for c in range(NC_TOK):
                    steps.do(dve.max_index(indices(c)[:, 8:16], values(c)[:, 8:16], cut_at(c)))

            def route_unit(layer, u):
                h, half = u // 2, u % 2
                idx = C0[f"wq{layer}"] + u
                dve.wait_ge(c_full, idx + 1)
                top16(lambda c: ps_c[idx % 2][:, c * P:(c + 1) * P], lambda c: top_v[:, c, h, half, :],
                      lambda c: top_i[:, c, h, half, :], lambda c: cut[:, c, :], c_free)
                if half == 0:
                    return
                steps.sync()
                for c in range(NC_TOK):
                    steps.do(dve.tensor_tensor(
                        cand[:, c, :].rearrange("p (a b) -> p a b", a=TOPK),
                        top_v[:, c, h, 0, :].unsqueeze(2).to_broadcast([P, TOPK, TOPK]),
                        top_v[:, c, h, 1, :].unsqueeze(1).to_broadcast([P, TOPK, TOPK]), ALU.add))
                steps.sync()
                top16(lambda c: cand[:, c, :], lambda c: sel_v[:, c, h, :], lambda c: sel_p[:, c, h, :],
                      lambda c: cand_cut[:, c, :])

            def start_decoding(layer):
                steps.sync()
                dve.wait_ge(c_free, GRANTED + C0[f"wq{layer}"] + 2 * PEER_HEADS)
                rows = sel_v[:].rearrange("p c h k -> p (c h) k")
                e = sel_f[:, 2, :, :].rearrange("p c (h k) -> p (c h) k", k=TOPK)
                dve.tensor_tensor(e, rows, rows[:, :, 0:1].to_broadcast([P, NC_TOK * PEER_HEADS, TOPK]),
                                  ALU.subtract).then_inc(soft_in, 1)
                flat = sel_p[:].rearrange("p c h k -> p (c h k)")
                steps.do(dve.tensor_scalar(pos_u[:, 0, :], flat, 4, None, ALU.logical_shift_right))
                steps.do(dve.tensor_scalar(pos_u[:, 1, :], flat, TOPK - 1, None, ALU.bitwise_and))
                steps.do(dve.tensor_copy(top_f[:].rearrange("p c h w k -> p (c h w k)"),
                                         top_i[:].rearrange("p c h w k -> p (c h w k)")))
                steps.sync()
                steps.do(dve.tensor_copy(pos_f[:].rearrange("p w s -> p (w s)"),
                                         pos_u[:].rearrange("p w s -> p (w s)")))
                steps.sync()

            def decode(w, k0, k_end):
                steps.sync()
                for k in range(k0, k_end):
                    steps.do(dve.scalar_tensor_tensor(
                        out=match[:, k, :].rearrange("p (h s) -> p h s", s=TOPK),
                        in0=pos_f[:, w, :].rearrange("p (h s) -> p h s", s=TOPK), scalar=float(k),
                        in1=top_f[:, :, :, w, k].rearrange("p c h -> p (c h)").unsqueeze(2).to_broadcast(
                            [P, NC_TOK * PEER_HEADS, TOPK]),
                        op0=ALU.is_equal, op1=ALU.mult))

            def sum_places(w, c):
                steps.sync()
                steps.do(dve.tensor_reduce(sel_f[:, w, c, :],
                                           match[:, :, c * P:(c + 1) * P].rearrange("p k s -> p s k"), AX.X, ALU.add))

            def finish_softmax(layer):
                n = NC_TOK * PEER_HEADS
                e = sel_f[:, 2, :, :].rearrange("p c (h k) -> p (c h) k", k=TOPK)
                dve.wait_ge(soft_out, layer + 1)
                steps.do(dve.tensor_reduce(soft[:, 0, 0:n], e, AX.X, ALU.add))
                steps.sync()
                steps.do(dve.reciprocal(soft[:, 1, 0:n], soft[:, 0, 0:n]))
                steps.sync()
                dve.tensor_tensor(e, e, soft[:, 1, 0:n].unsqueeze(2).to_broadcast([P, n, TOPK]),
                                  ALU.mult).then_inc(sel_ready, 1)

            def store_selections(layer):
                c0 = C0[f"sel{layer}"]
                dve.wait_ge(c_full, c0 + 1)
                dve.tensor_copy(i1_t[:], ps_c[c0 % 2][:, 0:S])
                dve.tensor_copy(i2_t[:], ps_c[c0 % 2][:, S:2 * S]).then_inc(c_free, 1)
                dve.wait_ge(c_full, c0 + 2)
                dve.tensor_scalar(g_full[:], ps_c[(c0 + 1) % 2][:, 0:S], WEIGHT_SCALE, None,
                                  ALU.mult).then_inc(c_free, 1)
                dve.wait_ge(c_free, GRANTED + c0 + 2)
                steps.do(dve.tensor_copy(g_parts[:, 0, :], g_full[:]))
                steps.sync()
                dve.tensor_tensor(g_parts[:, 1, :], g_full[:], g_parts[:, 0, :], ALU.subtract).then_inc(sel_t_ready, 1)
                dve.wait_ge(sel_t_ready, layer + 1)

            def peer(layer):
                base = U0[f"peer{layer}"]
                a0, b0, c0 = A0[f"peer{layer}"], B0[f"peer{layer}"], C0[f"peer{layer}"]
                done = layer * BATCHES

                def one_hots(b, it=None):
                    n = plus(b, it, BODY_BATCHES)
                    tok = (n % BATCHES_PER_Q) * BATCH
                    first = (n // BATCHES_PER_Q) * WQ_TILES
                    dve.wait_ge(c_full, plus(c0 + b - 1, it, BODY_BATCHES))
                    dve.tensor_tensor(hot2[:, b % 2, :, :], iota_rep[:],
                                      i2_t[:, bass.ds(tok, BATCH)].unsqueeze(1).to_broadcast([P, P, BATCH]),
                                      ALU.is_equal)
                    if it is not None or done + b > 0:
                        dve.wait_ge(hots_ready, plus(done + b, it, BODY_BATCHES))
                    dve.tensor_tensor(hot1[:], iota_rep[:, bass.ds(first, WQ_TILES), :],
                                      i1_t[:, bass.ds(tok, BATCH)].unsqueeze(1).to_broadcast([P, WQ_TILES, BATCH]),
                                      ALU.is_equal).then_inc(hot1_ready, 1)
                    dve.wait_ge(hot1_ready, plus(done + b + 1, it, BODY_BATCHES))
                    dve.tensor_tensor(hot1g[:, b % 2, :, :, :],
                                      hot1[:].unsqueeze(1).to_broadcast([P, 2, WQ_TILES, BATCH]),
                                      g_parts[:, :, bass.ds(tok, BATCH)].unsqueeze(2).to_broadcast(
                                          [P, 2, WQ_TILES, BATCH]), ALU.mult).then_inc(hots_ready, 1)

                def store_w(b, it=None):
                    n = plus(b, it, BODY_BATCHES)
                    tok = (n % BATCHES_PER_Q) * BATCH
                    slot = ((n // BATCHES_PER_Q) % 2) * WQ_TILES
                    dve.wait_ge(c_full, plus(c0 + b + 1, it, BODY_BATCHES))
                    dve.tensor_reduce(
                        w_route[:, bass.ds(slot, WQ_TILES), bass.ds(tok, BATCH)].rearrange("p i t -> p t i"),
                        ps_c[(c0 + b) % 2][:].rearrange("p (t w i) -> p t i w", w=2, i=WQ_TILES), AX.X,
                        ALU.add).then_inc(c_free, 1)

                def weigh(t, it=None, batches=None):
                    dve.wait_ge(gelu_done, plus(layer * TILES + t + 1, it, GROUP))
                    if batches is not None:
                        dve.wait_ge(c_free, batches)
                    st = stage[:, bass.ds(plus(t, it, GROUP) % AHEAD_TILES, 1), :]
                    dve.scalar_tensor_tensor(out=st, in0=w_route[:, bass.ds(plus(t, it, GROUP) % (2 * WQ_TILES), 1), :],
                                             scalar=1 / WEIGHT_SCALE, in1=st, op0=ALU.mult,
                                             op1=ALU.mult).then_inc(weighted, 1)

                def coefficients_lo(g, it=None, to=wa):
                    dve.wait_ge(wa_hi, plus(layer * GROUPS + g + 1, it, 1))
                    first = plus(g * GROUP, it, GROUP) % AHEAD_TILES
                    dve.tensor_tensor(to[:, :, 1, :], stage[:, bass.ds(first, GROUP), :], to[:, :, 0, :].bitcast(F32),
                                      ALU.subtract).then_inc(wa_lo, 1)

                def sum_tile(t, n0, it=None, per=0):
                    unit_done(dve, n0, it, per)
                    dst = stage[:, bass.ds(plus(t, it, GROUP) % AHEAD_TILES, 1), :].rearrange("p h t -> p (h t)")
                    sum_halves(dst, a0 + t)

                def build_at(b):
                    if b is not None:
                        store_w(b)
                        if b + 2 < PRE_BATCHES:
                            one_hots(b + 2)

                for j in range(AHEAD_TILES):
                    split_lo(base + j + LEAD)
                    if j == 1:
                        start_decoding(layer)
                    elif j == 2:
                        decode(0, 5, 10)
                    elif j == 3:
                        sum_places(0, 0)
                    elif j == 4:
                        decode(1, 0, 5)
                    elif j == 5:
                        decode(1, 11, TOPK)
                    elif j == 6:
                        sum_places(1, 1)
                    elif j == TURN_TILE:
                        store_selections(layer)
                    elif j == BUILD_TILE:
                        one_hots(1)
                    build_at(batch_at(j, 0))
                    sum_tile(j, base + j)
                    if j == 0:
                        route_unit(layer, 2 * PEER_HEADS - 1)
                    elif j == 1:
                        decode(0, 0, 5)
                    elif j == 2:
                        decode(0, 10, TOPK)
                    elif j == 3:
                        sum_places(0, 1)
                    elif j == 4:
                        decode(1, 5, 11)
                    elif j == 5:
                        sum_places(1, 0)
                    elif j == 6:
                        finish_softmax(layer)
                    elif j == TURN_TILE:
                        one_hots(0)
                    build_at(batch_at(j, 1))
                for j in range(GROUP):
                    weigh(j, batches=GRANTED + c0 + BATCHES_PER_Q)
                with nc.vector.Fori(0, FULL_BODIES) as i:
                    coefficients_lo(0, i)
                    for j in range(GROUP_UNITS):
                        split_lo(base + AHEAD_TILES + j + LEAD, i, GROUP_UNITS)
                        if j % 2 == 0:
                            one_hots(PRE_BATCHES + j // 2, i)
                        if j == 0:
                            dve.wait_ge(wa_lo, plus(layer * GROUPS + 1, i, 1))
                        if j < GROUP:
                            sum_tile(AHEAD_TILES + j, base + AHEAD_TILES + j, i, GROUP_UNITS)
                        if 1 <= j <= GROUP:
                            weigh(GROUP + j - 1, i,
                                  plus(GRANTED + c0 + PRE_BATCHES, i, BODY_BATCHES) if j == 1 else None)
                        if j >= GROUP:
                            q = j - GROUP
                            if j == GROUP:
                                dve.wait_ge(b_free, plus(GRANTED + b0, i, QUARTERS))
                            add_block(b0 + q, 512 * q, base + AHEAD_TILES + j, i, GROUP_UNITS)
                        if j == 1:
                            dve.wait_ge(weighted, plus(layer * TILES + GROUP, i, GROUP))
                        if j % 2 == 1:
                            store_w(PRE_BATCHES + j // 2, i)
                for g in range(FULL_BODIES, GROUPS):
                    first = base + TAIL + QUARTERS * (g - FULL_BODIES)
                    if g == FULL_BODIES:
                        coefficients_lo(g, to=tail_wa(g))
                    more = g + 1 < GROUPS
                    for q in range(QUARTERS):
                        split_lo(first + q + LEAD)
                        if more and q == 0:
                            for t in range(GROUP):
                                weigh((g + 1) * GROUP + t, batches=GRANTED + c0 + BATCHES)
                        if more and q == 2:
                            coefficients_lo(g + 1, to=tail_wa(g + 1))
                        if q == 0:
                            dve.wait_ge(b_free, GRANTED + b0 + g * QUARTERS)
                        add_block(b0 + QUARTERS * g + q, 512 * q, first + q)

            def routing(layer):
                w0, a0 = U0[f"wq{layer}"], A0[f"wq{layer}"]
                steps.do(dve.tensor_copy(iota_rep[:], iota[:].unsqueeze(2).to_broadcast([P, P, BATCH])))
                for u in range(2 * PEER_HEADS):
                    split_lo(w0 + u + LEAD)
                    if C0[f"wq{layer}"] + u - 1 > 0:
                        dve.wait_ge(c_full, C0[f"wq{layer}"] + u - 1)
                    unit_done(dve, w0 + u)
                    sum_halves(pq_t[:, u % 2, :], a0 + u)
                    if u >= 1:
                        route_unit(layer, u - 1)

            for s in (a_free, b_free, c_free):
                dve.sem_inc(s, GRANTED)
            dve.memset(eps_t[:], EPS).then_inc(dve_consts, 1)
            for m in range(LEAD):
                split_lo(m)
            scale_rows(0, lambda c: x_res[:, c, :], lambda c: xn[:, c, :], 0, xn_ready)
            dve.wait_ge(boot, 48)
            w = NC_TOK * HALF_ROPE
            pos_ff = soft[:, 0, 0:NC_TOK]
            steps.do(dve.tensor_copy(pos_ff, pos_i[:]))
            steps.sync()
            for c in range(NC_TOK):
                steps.do(dve.tensor_scalar(ang[:, 0, c * HALF_ROPE:(c + 1) * HALF_ROPE], invf[:],
                                           soft[:, 0, c:c + 1], None, ALU.mult))
            steps.sync()
            for shift, where in ((0.0, 4), (0.25, 5)):
                steps.do(dve.tensor_scalar(ang[:, 1, :], ang[:, 0, :], 1.0 / (2 * np.pi), shift, ALU.mult, ALU.add))
                steps.sync()
                steps.do(dve.tensor_scalar(ang[:, 1, :], ang[:, 1, :], ROUND, ROUND, ALU.add, ALU.subtract))
                steps.sync()
                src = ang[:, 0, :]
                for n, part in enumerate(TWO_PI_PARTS):
                    dst = ang[:, 2 + n % 2, :]
                    steps.do(dve.scalar_tensor_tensor(out=dst, in0=ang[:, 1, :], scalar=-part, in1=src,
                                                      op0=ALU.mult, op1=ALU.add))
                    steps.sync()
                    src = dst
                steps.do(dve.tensor_scalar(ang[:, where, :], src, 2 * np.pi * shift, None, ALU.add))
                steps.sync()
                steps.do(dve.tensor_scalar(ang[:, where, :], ang[:, where, :], PI_BELOW, -PI_BELOW, ALU.min, ALU.max))
                steps.sync()
            dve.sem_inc(angles, 1)
            gains_lo(A0["norm_sb"], KT, G_SB, act_t)

            dve.wait_ge(trig, 2)
            with nc.vector.Fori(0, 2 * HEADS // RAW_SLOTS) as i:
                for j in range(RAW_SLOTS):
                    split_lo(j + LEAD, i, RAW_SLOTS)
                    head = plus(j, i, RAW_SLOTS)
                    unit_done(dve, j, i, RAW_SLOTS)
                    dve.tensor_reduce(qk_t[:, bass.ds(head, 1), :].rearrange("p h t -> p (h t)"),
                                      ps_a[(A0["qk"] + j) % 2][:].rearrange("p (w t) -> p t w", w=2), AX.X,
                                      ALU.add).then_inc(a_free, 1)
            blocks(U0["v"], B0["v"], 4, lambda idx, col, last: copy_block(idx, v_tok, col, last))

            for h in range(HEADS + 2):
                if h < HEADS:
                    ps = ps_a[(A0["stick"] + h) % 2][:, 0:LIVE]
                    sp_, arg = st_sp[:, h % 2, :], st_arg[:, h % 2, :]
                    dve.wait_ge(a_full, AF0["stick"] + h + 1)
                    if h >= 2:
                        dve.wait_ge(st_exp, h - 1)
                    dve.tensor_scalar(arg, ps, SB_SCALE, None, ALU.mult).then_inc(a_free, 1)
                    dve.wait_ge(a_free, GRANTED + A0["stick"] + h + 1)
                    if h >= 2:
                        dve.wait_ge(st_masked, h - 1)
                    steps.do(dve.tensor_scalar(sp_, arg, 0.0, None, ALU.max))
                    steps.sync()
                    dve.wait_ge(st_log, h + 1)
                    dve.tensor_tensor(sp_, sp_, st_l[:, h % 2, :], ALU.add).then_inc(st_soft, 1)
                    dve.wait_ge(st_soft, h + 1)
                    steps.do(dve.tensor_tensor(arg, arg, sp_, ALU.subtract))
                if 1 <= h <= HEADS:
                    g = h - 1
                    arg = st_arg[:, g % 2, :]
                    dve.wait_ge(c_full, C0["stick"] + g + 1)
                    steps.sync()
                    dve.tensor_tensor(arg, arg, ps_c[(C0["stick"] + g) % 2][:, 0:LIVE],
                                      ALU.subtract).then_inc(st_args, 1)
                    dve.wait_ge(st_args, g + 1)
                    dve.sem_inc(c_free, 1)
                if h >= 2:
                    output_lo(h - 2, B0["stick"], 0)
            blocks(U0["wo"], B0["wo"], 4, add_block)

            def block_norm(k, a0, col):
                scale_rows(k, lambda c: x_res[:, c, :], lambda c: xn[:, c, :], 0, xn_ready)
                gains_lo(a0, KT, col, act_t)

            block_norm(1, A0["norm_p0"], G_P0)
            routing(0)
            peer(0)

            block_norm(2, A0["norm_kv"], G_KV)
            for n in range(U0["c"], U0["rope"] + 1):
                split_lo(n + LEAD)
            gains_lo(A0["norm_mla"], KT, G_MLA, act_t)
            c_idx, r_idx = B0["c"], B0["rope"]
            unit_done(dve, U0["c"] + 3)
            scale_rows(3, lambda c: ps_b[c_idx % 2][c][:], lambda c: c_tok[:, c, :], 4, xn_ready)
            dve.wait_ge(xn_ready, 4)
            dve.sem_inc(b_free, 1)
            unit_done(dve, U0["rope"])
            for c in range(NC_TOK):
                for twice in range(2):
                    rotate(ps_b[r_idx % 2][c][:, 0:ROPE].unsqueeze(1),
                           kr_tok[:, c, twice * ROPE:(twice + 1) * ROPE].unsqueeze(1), c, 1)
            dve.sem_inc(kr_ready, 1)
            dve.sem_inc(b_free, 1)
            gains_lo(A0["ct"], LT, G_LKV, c_t)
            dve.wait_ge(a_full, AF0["krt"] + 1)
            dve.tensor_copy(kr_t[:], ps_a[A0["krt"] % 2][:, 0:S]).then_inc(a_free, 1)
            for n in range(U0["dq"], U0["kn"]):
                split_lo(n + LEAD)
            d_idx = B0["dq"]
            unit_done(dve, U0["dq"] + 3)
            scale_rows(4, lambda c: ps_b[d_idx % 2][c][:], lambda c: c_tok[:, c, :], 8, xn_ready)
            dve.wait_ge(xn_ready, 5)
            dve.sem_inc(b_free, 1)

            def head_products(phase, dst):
                first = U0[phase]
                for n in range(HEADS // 4):
                    for j, s, k in halves(first + n, None, 0):
                        dve.wait_ge(a_full, AF0[phase] + 2 * n + j + 1)
                        sum_halves(dst[:, 4 * n + 2 * j, :], A0[phase] + 4 * n + 2 * j)
                        dve.wait_ge(used[s], k + 1)
                        sum_halves(dst[:, 4 * n + 2 * j + 1, :], A0[phase] + 4 * n + 2 * j + 1)
                    split_lo(first + n + LEAD)

            head_products("kn", kn_t)
            for nb in range(4):
                split_lo(U0["mv"] + nb + LEAD)
                copy_block(B0["mv"] + nb, mv_tok, 512 * nb, U0["mv"] + nb)
            gains_lo(A0["cqt"], LT, G_LQ, cq_t)
            head_products("uqn", qn_t)
            for nb in range(2):
                split_lo(U0["uqr"] + nb + LEAD)
                idx = B0["uqr"] + nb
                unit_done(dve, U0["uqr"] + nb)
                for c in range(NC_TOK):
                    rotate(ps_b[idx % 2][c][:].rearrange("p (h f) -> p h f", f=ROPE),
                           qr_tok[:, c, 512 * nb:512 * (nb + 1)].rearrange("p (h f) -> p h f", f=ROPE), c, 8)
                dve.sem_inc(b_free, 1)
            dve.sem_inc(qr_ready, 1)
            for f in range(4):
                idx = A0["qrt"] + f
                dve.wait_ge(a_full, AF0["qrt"] + f + 1)
                dve.tensor_copy(qr_t[:, 2 * f:2 * f + 2, :].rearrange("p h t -> p (h t)"),
                                ps_a[idx % 2][:]).then_inc(a_free, 1)
            for h in range(HEADS + 2):
                if h < HEADS:
                    idx = A0["mla"] + h
                    s_, m_ = ml_s[:, h % 2, :], ml_stat[:, h % 2, :]
                    dve.wait_ge(a_full, AF0["mla"] + h + 1)
                    if h >= 2:
                        dve.wait_ge(ml_exp, h - 1)
                    outer = s_.rearrange("p (b k) -> p b k", b=3)[:, 0:3:2, :]
                    outer_ps = ps_a[idx % 2][:, 0:LIVE].rearrange("p (b k) -> p b k", b=3)[:, 0:3:2, :]
                    steps.do(dve.tensor_tensor(outer, outer_ps, neg_upper[:].unsqueeze(1).to_broadcast([P, 2, P]),
                                               ALU.add))
                    dve.tensor_copy(s_[:, P:2 * P], ps_a[idx % 2][:, P:2 * P]).then_inc(a_free, 1)
                    steps.sync()
                    dve.wait_ge(a_free, GRANTED + idx + 1)
                    steps.do(dve.tensor_reduce(m_[:, 0:1], s_[:, 0:P], AX.X, ALU.max))
                    steps.do(dve.tensor_reduce(m_[:, 1:2], s_[:, P:LIVE], AX.X, ALU.max))
                    steps.sync()
                    dve.tensor_scalar(m_[:, 2:4], m_[:, 0:2], -MLA_SCALE, None, ALU.mult).then_inc(ml_masked, 1)
                if 1 <= h <= HEADS:
                    g = h - 1
                    m_ = ml_stat[:, g % 2, :]
                    dve.wait_ge(ml_exp, g + 1)
                    steps.do(dve.reciprocal(m_[:, 6:8], m_[:, 4:6]))
                    steps.sync()
                    for c, (lo_col, hi_col) in enumerate(((0, P), (P, LIVE))):
                        pr = ml_p[:, g % 2, lo_col:hi_col]
                        ins = dve.tensor_scalar(pr, pr, m_[:, 6 + c:7 + c], None, ALU.mult)
                    ins.then_inc(ml_norm, 1)
                if h >= 2:
                    output_lo(h - 2, B0["mla"], HEADS)
            blocks(U0["mwo"], B0["mwo"], 4, add_block)

            block_norm(5, A0["norm_p1"], G_P1)
            routing(1)
            peer(1)

            dve.wait_ge(stds, 7)
            steps.do(dve.reciprocal(stat[:, 2:4], stat[:, 0:2]))
            steps.sync()
            dve.wait_ge(gain_row_in, 16)
            for c in range(NC_TOK):
                dve.scalar_tensor_tensor(out=xn[:, c, :], in0=x_res[:, c, :], scalar=stat[:, 2 + c:3 + c],
                                         in1=gain_row[:], op0=ALU.mult, op1=ALU.mult).then_inc(final_ready, 1)

        @block.tensor
        def _(pe):
            mm = pe.matmul

            def weights_by_features(n0, ps, it=None, per=0, middle=None):
                for j, s, k in halves(n0, it, per):
                    pe.wait_ge(lo_ready[s], k + 1)
                    if j and middle:
                        middle()
                    for q in range(KT // 2):
                        kt = KT // 2 * j + q
                        w_hi, w_lo = (t[:, s, q * P:(q + 1) * P] for t in (hi, lo))
                        first, last = kt == 0, kt == KT - 1
                        if not first:
                            mm(ps[:, 0:S], w_lo, act_t[:, kt, 0, :], start=False, stop=False, skip_group_check=True)
                        ins = mm(ps[:], w_hi, act_t[:, kt, :, :].rearrange("p w t -> p (w t)"), start=first, stop=last)
                        if first:
                            ins = mm(ps[:, 0:S], w_lo, act_t[:, kt, 0, :], start=False, stop=False,
                                     skip_group_check=True)
                    ins.then_inc(used[s], 1)

            def unit_a(n0, idx, it=None, per=0, a_per=0, middle=None):
                pe.wait_ge(a_free, plus(idx + 1, it, a_per))
                weights_by_features(n0, ps_a[idx % 2], it, per, middle)

            def tokens_by_columns(n0, pair, act, kt0, kt_end, it=None, per=0, width=512, k_tiles=2):
                for j, s, k in halves(n0, it, per):
                    pe.wait_ge(lo_ready[s], k + 1)
                    for q in range(k_tiles):
                        kt = kt0 + k_tiles * j + q
                        w_hi, w_lo = (t[:, s, q * width:(q + 1) * width] for t in (hi, lo))
                        for c in range(NC_TOK):
                            a_hi, a_lo = (act[:, kt, w, c * P:(c + 1) * P] for w in range(2))
                            o = pair[c][:, 0:width]
                            mm(o, a_hi, w_hi, start=(kt == 0), stop=False)
                            mm(o, a_hi, w_lo, start=False, stop=False)
                            ins = mm(o, a_lo, w_hi, start=False, stop=(kt == kt_end - 1))
                    ins.then_inc(used[s], 1)

            def block_b(n0, idx, act, n_units, it=None, per=0, b_per=0):
                pe.wait_ge(b_free, plus(idx + 1, it, b_per))
                for u in range(n_units):
                    tokens_by_columns(n0 + u, ps_b[idx % 2], act, 4 * u, 4 * n_units, it, per)

            def turn(blocks_, a0):
                for f in range((len(blocks_) + 3) // 4):
                    idx = a0 + f
                    pe.wait_ge(a_free, idx + 1)
                    for q, blk in enumerate(blocks_[4 * f:4 * f + 4]):
                        ins = pe.transpose(ps_a[idx % 2][:, q * P:(q + 1) * P], blk, ident[:])
                    ins.then_inc(a_full, 1)

            def turn_rows(rows, k_tiles, a0):
                turn([rows[:, c, kt * P:(kt + 1) * P] for kt in range(k_tiles) for c in range(NC_TOK)], a0)

            def norm(count, a0):
                pe.wait_ge(xn_ready, count)
                turn_rows(xn, KT, a0)
                pe.wait_ge(a_free, GRANTED + a0 + KT // 2)

            def head_products(first, a0, act):
                for n in range(HEADS // 4):
                    for j, s, k in halves(first + n, None, 0):
                        pe.wait_ge(lo_ready[s], k + 1)
                        for m in range(2):
                            idx = a0 + 4 * n + 2 * j + m
                            pe.wait_ge(a_free, idx + 1)
                            ps = ps_a[idx % 2]
                            for kt in range(LT):
                                at = (LT * m + kt) * P
                                w_hi, w_lo = (t[:, s, at:at + P] for t in (hi, lo))
                                last = kt == LT - 1
                                if not last:
                                    mm(ps[:], w_hi, act[:, kt, :, :].rearrange("p w t -> p (w t)"), start=(kt == 0),
                                       stop=False, skip_group_check=True)
                                mm(ps[:, 0:S], w_lo, act[:, kt, 0, :], start=False, stop=False, skip_group_check=True)
                                if last:
                                    ins = mm(ps[:], w_hi, act[:, kt, :, :].rearrange("p w t -> p (w t)"), start=False,
                                             stop=True, skip_group_check=True)
                            ins.then_inc(a_full if m == 0 else used[s], 1)

            def head_outputs(idx, h, v, w):
                v0, v1 = (v[:, c, h * P:(h + 1) * P] for c in range(NC_TOK))
                ps = ps_b[idx % 2][0]
                mm(ps[:, 0:P], v0, w[:, 0:P], start=True, stop=True)
                mm(ps[:, P:S], v0, w[:, P:2 * P], start=True, stop=False)
                mm(ps[:, P:S], v1, w[:, 2 * P:LIVE], start=False, stop=True).then_inc(b_full, 1)

            def keys_product(layer, u):
                idx = C0[f"wq{layer}"] + u
                pe.wait_ge(a_free, GRANTED + A0[f"wq{layer}"] + u + 1)
                pe.wait_ge(keys_in, 16 * (layer + 1))
                pe.wait_ge(c_free, idx + 1)
                for c in range(NC_TOK):
                    ins = mm(ps_c[idx % 2][:, c * P:(c + 1) * P], pq_t[:, u % 2, c * P:(c + 1) * P], keys_sb[:, u, :],
                             start=True, stop=True)
                ins.then_inc(c_full, 1)

            def peer(layer):
                base = U0[f"peer{layer}"]
                a0, b0, c0 = A0[f"peer{layer}"], B0[f"peer{layer}"], C0[f"peer{layer}"]

                def build_w(b, it=None):
                    count = plus(layer * BATCHES + b + 1, it, BODY_BATCHES)
                    pe.wait_ge(hots_ready, count)
                    for t in range(BATCH):
                        ins = mm(ps_c[(c0 + b) % 2][:, t * 2 * WQ_TILES:(t + 1) * 2 * WQ_TILES],
                                 hot2[:, b % 2, :, t], hot1g[:, b % 2, :, :, t].rearrange("p w i -> p (w i)"),
                                 start=True, stop=True)
                    ins.then_inc(c_full, 1)

                def turn_selections():
                    pe.wait_ge(sel_ready, layer + 1)
                    blocks_ = [sel_f[:, w, c, :] for w in range(3) for c in range(NC_TOK)]
                    for f, some in enumerate((blocks_[0:4], blocks_[4:6])):
                        idx = C0[f"sel{layer}"] + f
                        pe.wait_ge(c_free, idx + 1)
                        for q, blk in enumerate(some):
                            ins = pe.transpose(ps_c[idx % 2][:, q * P:(q + 1) * P], blk, ident[:])
                        ins.then_inc(c_full, 1)

                for j in range(AHEAD_TILES):
                    mid, end = batch_at(j, 0), batch_at(j, 1)
                    if j == 0:
                        unit_a(base + j, a0 + j, middle=lambda: keys_product(layer, 2 * PEER_HEADS - 1))
                    elif j == TURN_TILE:
                        unit_a(base + j, a0 + j, middle=turn_selections)
                    else:
                        unit_a(base + j, a0 + j, middle=(lambda b=mid: build_w(b)) if mid is not None else None)
                    if end is not None:
                        build_w(end)
                with nc.tensor.Fori(0, FULL_BODIES) as i:
                    for j in range(GROUP_UNITS):
                        if j < GROUP:
                            unit_a(base + AHEAD_TILES + j, a0 + AHEAD_TILES + j, i, GROUP_UNITS, GROUP)
                        else:
                            if j == GROUP:
                                pe.wait_ge(wa_lo, plus(layer * GROUPS + 1, i, 1))
                            block_b(base + AHEAD_TILES + j, b0 + j - GROUP, wa, 1, i, GROUP_UNITS, QUARTERS)
                        if j % 2 == 1:
                            build_w(PRE_BATCHES + j // 2, i)
                for g in range(FULL_BODIES, GROUPS):
                    pe.wait_ge(wa_lo, layer * GROUPS + g + 1)
                    for q in range(QUARTERS):
                        block_b(base + TAIL + QUARTERS * (g - FULL_BODIES) + q, b0 + QUARTERS * g + q, tail_wa(g), 1)

            def routing(layer):
                for u in range(2 * PEER_HEADS):
                    unit_a(U0[f"wq{layer}"] + u, A0[f"wq{layer}"] + u,
                           middle=(lambda u=u: keys_product(layer, u - 1)) if u else None)

            pe.wait_ge(consts, N_CONSTS)
            norm(1, A0["norm_sb"])
            with nc.tensor.Fori(0, 2 * HEADS // RAW_SLOTS) as i:
                for j in range(RAW_SLOTS):
                    unit_a(j, A0["qk"] + j, i, RAW_SLOTS, RAW_SLOTS)
            for nb in range(4):
                block_b(U0["v"] + 4 * nb, B0["v"] + nb, act_t, 4)

            pe.wait_ge(a_free, GRANTED + A0["qk"] + 2 * HEADS)
            pe.wait_ge(b_free, GRANTED + B0["v"] + 4)
            for h in range(HEADS + 2):
                if h < HEADS:
                    idx = A0["stick"] + h
                    pe.wait_ge(a_free, idx + 1)
                    qh, kh = qk_t[:, h, :], qk_t[:, HEADS + h, :]
                    mm(ps_a[idx % 2][:, 0:S], kh[:, 0:P], qh, start=True, stop=True)
                    mm(ps_a[idx % 2][:, S:LIVE], kh[:, P:S], qh[:, P:S], start=True, stop=True).then_inc(a_full, 1)
                if 1 <= h <= HEADS:
                    g = h - 1
                    idx = C0["stick"] + g
                    ps, m = ps_c[idx % 2], st_spm[:, g % 2, :]
                    pe.wait_ge(c_free, idx + 1)
                    pe.wait_ge(st_masked, g + 1)
                    mm(ps[:, 0:P], tri[:], m[:, 0:P], start=True, stop=True)
                    mm(ps[:, P:2 * P], tri[:], m[:, P:2 * P], start=True, stop=False)
                    mm(ps[:, P:2 * P], ones[:], m[:, 2 * P:LIVE], start=False, stop=True)
                    mm(ps[:, 2 * P:LIVE], tri[:], m[:, 2 * P:LIVE], start=True, stop=True).then_inc(c_full, 1)
                if h >= 2:
                    g = h - 2
                    pe.wait_ge(b_free, B0["stick"] + g + 1)
                    pe.wait_ge(st_weights, g + 1)
                    head_outputs(B0["stick"] + g, g, v_tok, st_a[:, g % 2, :])
            pe.wait_ge(b_free, GRANTED + B0["stick"] + HEADS)
            for nb in range(4):
                block_b(U0["wo"] + 4 * nb, B0["wo"] + nb, act_t, 4)

            norm(2, A0["norm_p0"])
            routing(0)
            peer(0)

            norm(3, A0["norm_kv"])
            block_b(U0["c"], B0["c"], act_t, 4)
            pe.wait_ge(b_free, B0["rope"] + 1)
            n = U0["rope"]
            (_, s0, k0), (_, s1, k1) = halves(n, None, 0)
            pe.wait_ge(lo_ready[s0], k0 + 1)
            for kt in range(KT):
                w_hi, w_lo = (t[:, s0, kt * ROPE:(kt + 1) * ROPE] for t in (hi, lo))
                for c in range(NC_TOK):
                    a_hi, a_lo = (act_t[:, kt, w, c * P:(c + 1) * P] for w in range(2))
                    o = ps_b[B0["rope"] % 2][c][:, 0:ROPE]
                    mm(o, a_hi, w_hi, start=(kt == 0), stop=False)
                    mm(o, a_hi, w_lo, start=False, stop=False)
                    ins = mm(o, a_lo, w_hi, start=False, stop=(kt == KT - 1))
            ins.then_inc(used[s0], 1)
            pe.wait_ge(used[s0], k0 + 1)
            pe.wait_ge(lo_ready[s1], k1 + 1)
            pe.sem_inc(used[s1], 1)
            turn_rows(xn, KT, A0["norm_mla"])
            pe.wait_ge(xn_ready, 4)
            turn_rows(c_tok, LT, A0["ct"])
            pe.wait_ge(kr_ready, 1)
            turn([kr_tok[:, c, :] for c in range(NC_TOK)], A0["krt"])
            pe.wait_ge(a_free, GRANTED + A0["krt"] + 1)
            block_b(U0["dq"], B0["dq"], act_t, 4)
            head_products(U0["kn"], A0["kn"], c_t)
            for nb in range(4):
                block_b(U0["mv"] + nb, B0["mv"] + nb, c_t, 1)
            pe.wait_ge(xn_ready, 5)
            turn_rows(c_tok, LT, A0["cqt"])
            pe.wait_ge(a_free, GRANTED + A0["cqt"] + 2)
            head_products(U0["uqn"], A0["uqn"], cq_t)
            for nb in range(2):
                block_b(U0["uqr"] + nb, B0["uqr"] + nb, cq_t, 1)
            pe.wait_ge(qr_ready, 1)
            turn([qr_tok[:, c, h * P:(h + 1) * P] for h in range(HEADS // 2) for c in range(NC_TOK)], A0["qrt"])
            pe.wait_ge(a_free, GRANTED + A0["qrt"] + 4)
            pe.wait_ge(b_free, GRANTED + B0["mv"] + 4)
            for h in range(HEADS + 2):
                if h < HEADS:
                    idx = A0["mla"] + h
                    ps, r = ps_a[idx % 2], slice(ROPE * (h % 2), ROPE * (h % 2 + 1))
                    pe.wait_ge(a_free, idx + 1)
                    for o, q, keys_of in ((slice(0, P), slice(0, P), slice(0, P)),
                                          (slice(P, LIVE), slice(P, S), slice(0, S))):
                        mm(ps[:, o], qn_t[:, h, q], kn_t[:, h, keys_of], start=True, stop=False)
                        ins = mm(ps[:, o], qr_t[r, h // 2, q], kr_t[r, keys_of], start=False, stop=True)
                    ins.then_inc(a_full, 1)
                if 1 <= h <= HEADS:
                    g = h - 1
                    idx = C0["mla"] + g
                    pe.wait_ge(c_free, idx + 1)
                    pe.wait_ge(ml_norm, g + 1)
                    for b in range(3):
                        ins = pe.transpose(ps_c[idx % 2][:, b * P:(b + 1) * P], ml_p[:, g % 2, b * P:(b + 1) * P],
                                           ident[:])
                    ins.then_inc(c_full, 1)
                if h >= 2:
                    g = h - 2
                    pe.wait_ge(b_free, B0["mla"] + g + 1)
                    pe.wait_ge(c_free, GRANTED + C0["mla"] + g + 1)
                    head_outputs(B0["mla"] + g, g, mv_tok, ml_pt[:, g % 2, :])
            pe.wait_ge(b_free, GRANTED + B0["mla"] + HEADS)
            for nb in range(4):
                block_b(U0["mwo"] + 4 * nb, B0["mwo"] + nb, act_t, 4)

            norm(6, A0["norm_p1"])
            routing(1)
            peer(1)


def unit_features(w):
    k, n = w.shape
    return w.reshape(k // P, P, n // P, P).transpose(2, 1, 0, 3).reshape(n // P, P, UNIT)


def unit_columns(w):
    k, n = w.shape
    return w.reshape(k // (4 * P), 4, P, n // 512, 512).transpose(3, 0, 2, 1, 4).reshape(-1, P, UNIT)


def unit_heads(w):
    return w.reshape(LT, P, HEADS // 4, 4, P).transpose(2, 1, 3, 0, 4).reshape(HEADS // 4, P, UNIT)


def unit_experts(out, u, v):
    ut = u.reshape(TILES, P, KT, P).transpose(0, 3, 2, 1).reshape(GROUPS, GROUP, P, UNIT)
    vt = v.reshape(GROUPS, GROUP, P, QUARTERS, 512).transpose(0, 3, 2, 1, 4).reshape(GROUPS, QUARTERS, P, UNIT)
    out[0:AHEAD_TILES] = ut[:AHEAD].reshape(AHEAD_TILES, P, UNIT)
    body = out[AHEAD_TILES:TAIL].reshape(FULL_BODIES, GROUP_UNITS, P, UNIT)
    body[:, 0:GROUP] = ut[AHEAD:]
    body[:, GROUP:] = vt[:FULL_BODIES]
    out[TAIL:] = vt[FULL_BODIES:].reshape(AHEAD * QUARTERS, P, UNIT)


def kernel(**inputs):
    import concourse.bacc as bacc
    from concourse.bass_utils import run_bass_kernel_spmd

    a = {k: np.asarray(v) for k, v in inputs.items()}
    qkv = a["sb_w_qkv"][0]
    ukv = a["mla_w_ukv"].reshape(LORA, HEADS, 2 * P)
    uq = a["mla_w_uq"][0].reshape(LORA, HEADS, P + ROPE)
    rope_unit = np.zeros((1, P, UNIT), np.float32)
    rope_unit[0, :, 0:KT * ROPE] = (a["mla_w_dkv"][:, LORA:].reshape(KT, P, ROPE).transpose(1, 0, 2)
                                    .reshape(P, KT * ROPE))
    parts = {
        "qk": unit_features(qkv[:, :2 * D]), "v": unit_columns(qkv[:, 2 * D:]), "wo": unit_columns(a["sb_w_o"][0]),
        "wq0": unit_features(a["peer_w_q"][0]), "c": unit_columns(a["mla_w_dkv"][:, :LORA]), "rope": rope_unit,
        "dq": unit_columns(a["mla_w_dq"][0]), "kn": unit_heads(ukv[:, :, :P]),
        "mv": unit_columns(ukv[:, :, P:].reshape(LORA, D)), "uqn": unit_heads(uq[:, :, :P]),
        "uqr": unit_columns(uq[:, :, P:].reshape(LORA, HEADS * ROPE)), "mwo": unit_columns(a["mla_w_o"][0]),
        "wq1": unit_features(a["peer_w_q"][1]),
    }
    stream = np.empty((N_UNITS, P, UNIT), np.float32)
    for name, count in PHASE_UNITS:
        dst = stream[U0[name]:U0[name] + count]
        if name in parts:
            dst[:] = parts[name]
        else:
            layer = int(name[-1])
            unit_experts(dst, a["peer_u"][layer], a["peer_v"][layer])
    keys = np.stack([a["peer_keys_1"], a["peer_keys_2"]], axis=2)
    keys = np.ascontiguousarray(keys.transpose(0, 4, 1, 2, 3).reshape(2, P, 2 * PEER_HEADS * NKEYS))
    gains = np.concatenate([g.reshape(-1, P) for g in (
        a["sb_norm_g"][0], a["peer_norm_g"][0], a["kv_norm_g"], a["mla_norm_g"][0], a["peer_norm_g"][1],
        a["mla_kv_latent_g"], a["mla_q_latent_g"][0])]).T
    arrays = {
        "x": a["x"][0], "positions": a["positions"].reshape(NC_TOK, P).T, "stream": stream, "keys": keys,
        "gains": gains, "final_g": a["final_norm_g"].reshape(1, D),
        "inv_freq": (np.float32(10000.0) ** (-np.arange(0, ROPE, 2, dtype=np.float32) / ROPE)).reshape(1, HALF_ROPE),
    }
    arrays = {f"in_{k}": np.ascontiguousarray(v) for k, v in arrays.items()}
    nc = bacc.Bacc("TRN2", target_bir_lowering=False, num_devices=1)
    aps = {k[3:]: nc.dram_tensor(k, v.shape, mybir.dt.from_np(v.dtype), kind="ExternalInput").ap()
           for k, v in arrays.items()}
    out = nc.dram_tensor("out", (S, D), F32, kind="ExternalOutput").ap()
    build_program(nc, out=out, **aps)
    result = run_bass_kernel_spmd(nc, [arrays], core_ids=[0])
    return result.results[0]["out"].reshape(1, S, D)
```
